# Optimizing a Trainium2 kernel written in Bass

```python
import jax, jax.numpy as jnp
from jax import lax
import numpy as np

D_MODEL = 1024
BATCH = 1
SEQ = 512
DEPTH = 1

GRID_W = 64
MEM_LEN = 256
HEAD_DIM = 64
NA_HEADS = 8
NA_WIDTH = NA_HEADS * HEAD_DIM
CONV_WIDTH = D_MODEL - NA_WIDTH
MIX_WIDTH = NA_WIDTH + CONV_WIDTH
CONV_K = 3
NA_WIN_ROWS = 8
NA_WIN_COLS = 16
MEM_HEADS = 4
MEM_HEAD_DIM = 128
MEM_WIDTH = MEM_HEADS * MEM_HEAD_DIM
N_EXPERTS = 16
EC_CAPACITY_FACTOR = 2
EXPERT_FF = 2048
LN_EPS = 1e-5
DN_ALPHA = (2 * DEPTH) ** 0.25
DN_BETA = (8 * DEPTH) ** -0.25

kernel_name = "hybrid_na2d_shortconv_memxattn_ecmoe"

def layer_norm(x, g, b):
    xf = x.astype(jnp.float32)
    mu = jnp.mean(xf, axis=-1, keepdims=True)
    var = jnp.mean(jnp.square(xf - mu), axis=-1, keepdims=True)
    return ((xf - mu) * lax.rsqrt(var + LN_EPS)).astype(x.dtype) * g + b

def window_starts(n, win):
    return jnp.clip(jnp.arange(n) - win // 2, 0, n - win)

def neighbourhood_attention(q, k, v, rpb):
    B, S, H, Dh = q.shape
    rows = S // GRID_W
    kr = min(NA_WIN_ROWS, rows)
    kc = NA_WIN_COLS
    qg = q.reshape(B, rows, GRID_W, H, Dh)
    kg = k.reshape(B, rows, GRID_W, H, Dh)
    vg = v.reshape(B, rows, GRID_W, H, Dh)
    row_idx = window_starts(rows, kr)[:, None] + jnp.arange(kr)[None, :]
    k_rows = kg[:, row_idx]
    v_rows = vg[:, row_idx]
    scores = jnp.einsum('brqhd,brjkhd->bhrqjk', qg, k_rows,
                        preferred_element_type=jnp.float32) * (Dh ** -0.5)
    dr_idx = row_idx - jnp.arange(rows)[:, None] + (NA_WIN_ROWS - 1)
    cols = jnp.arange(GRID_W)
    dc = cols[None, :] - cols[:, None]
    dc_idx = jnp.clip(dc, -(kc - 1), kc - 1) + (kc - 1)
    c_start = window_starts(GRID_W, kc)[:, None]
    col_mask = (cols[None, :] >= c_start) & (cols[None, :] < c_start + kc)
    bias = rpb[:, dr_idx[:, None, :, None], dc_idx[None, :, None, :]]
    scores = scores + bias[None].astype(jnp.float32)
    scores = jnp.where(col_mask[:, None, :], scores, jnp.finfo(jnp.float32).min)
    probs = jax.nn.softmax(scores.reshape(B, H, rows, GRID_W, kr * GRID_W), axis=-1)
    probs = probs.reshape(B, H, rows, GRID_W, kr, GRID_W).astype(v.dtype)
    out = jnp.einsum('bhrqjk,brjkhd->brqhd', probs, v_rows)
    return out.reshape(B, S, H * Dh)

def short_conv(u, w):
    rhs = w[:, None, :].astype(u.dtype)
    return lax.conv_general_dilated(u, rhs, window_strides=(1,),
                                    padding=[(CONV_K // 2, CONV_K // 2)],
                                    dimension_numbers=('NWC', 'WIO', 'NWC'),
                                    feature_group_count=u.shape[-1])

def hybrid_mixer(x, w_in, rpb, conv_w, w_out):
    B, S, _ = x.shape
    proj = x @ w_in
    splits = [NA_WIDTH, 2 * NA_WIDTH, 3 * NA_WIDTH,
              3 * NA_WIDTH + CONV_WIDTH, 3 * NA_WIDTH + 2 * CONV_WIDTH]
    q, k, v, b_gate, c_gate, h = jnp.split(proj, splits, axis=-1)
    heads = lambda t: t.reshape(B, S, NA_HEADS, HEAD_DIM)
    y_na = neighbourhood_attention(heads(q), heads(k), heads(v), rpb)
    y_conv = b_gate * short_conv(c_gate * h, conv_w)
    return jnp.concatenate([y_na, y_conv], axis=-1) @ w_out

def memory_cross_attention(x, mem, wq, wk, wv, wo):
    B, S, _ = x.shape
    M = mem.shape[1]
    q = (x @ wq).reshape(B, S, MEM_HEADS, MEM_HEAD_DIM)
    k = (mem @ wk).reshape(B, M, MEM_HEADS, MEM_HEAD_DIM)
    v = (mem @ wv).reshape(B, M, MEM_HEADS, MEM_HEAD_DIM)
    s = jnp.einsum('bshd,bmhd->bhsm', q, k,
                   preferred_element_type=jnp.float32) * (MEM_HEAD_DIM ** -0.5)
    p = jax.nn.softmax(s, axis=-1).astype(v.dtype)
    o = jnp.einsum('bhsm,bmhd->bshd', p, v).reshape(B, S, MEM_WIDTH)
    return o @ wo

def expert_choice_moe(x, w_router, w_gate, w_up, w_down):
    B, S, D = x.shape
    cap = EC_CAPACITY_FACTOR * S // N_EXPERTS
    logits = jnp.einsum('bsd,de->bse', x, w_router, preferred_element_type=jnp.float32)
    affinity = jax.nn.softmax(logits, axis=-1)
    gates, idx = lax.top_k(jnp.swapaxes(affinity, 1, 2), cap)
    xe = jax.vmap(lambda xb, ib: xb[ib])(x, idx)
    hid = jax.nn.silu(jnp.einsum('becd,edf->becf', xe, w_gate)) * \
        jnp.einsum('becd,edf->becf', xe, w_up)
    ye = jnp.einsum('becf,efd->becd', hid, w_down) * gates[..., None].astype(x.dtype)
    scatter = lambda ib, yb: jnp.zeros((S, D), yb.dtype).at[ib.reshape(-1)].add(yb.reshape(-1, D))
    return jax.vmap(scatter)(idx, ye)

def setup_inputs(seed: int = 0) -> dict:
    key = jax.random.key(seed)
    ks = jax.random.split(key, 20)
    nrm = lambda k, shape, scale: jax.random.normal(k, shape, jnp.float32) * scale
    L = DEPTH
    return {
        "x": nrm(ks[0], (BATCH, SEQ, D_MODEL), 1.0),
        "mem": nrm(ks[1], (BATCH, MEM_LEN, D_MODEL), 1.0),
        "w_in": nrm(ks[2], (L, D_MODEL, 3 * NA_WIDTH + 3 * CONV_WIDTH), D_MODEL ** -0.5),
        "na_rpb": nrm(ks[3], (L, NA_HEADS, 2 * NA_WIN_ROWS - 1, 2 * NA_WIN_COLS - 1), 0.1),
        "conv_w": nrm(ks[4], (L, CONV_K, CONV_WIDTH), CONV_K ** -0.5),
        "w_mix_out": nrm(ks[5], (L, MIX_WIDTH, D_MODEL), MIX_WIDTH ** -0.5 * DN_BETA),
        "ln1_g": 1.0 + nrm(ks[6], (L, D_MODEL), 0.02),
        "ln1_b": nrm(ks[7], (L, D_MODEL), 0.02),
        "w_mem_q": nrm(ks[8], (L, D_MODEL, MEM_WIDTH), D_MODEL ** -0.5),
        "w_mem_k": nrm(ks[9], (L, D_MODEL, MEM_WIDTH), D_MODEL ** -0.5),
        "w_mem_v": nrm(ks[10], (L, D_MODEL, MEM_WIDTH), D_MODEL ** -0.5),
        "w_mem_out": nrm(ks[11], (L, MEM_WIDTH, D_MODEL), MEM_WIDTH ** -0.5 * DN_BETA),
        "ln2_g": 1.0 + nrm(ks[12], (L, D_MODEL), 0.02),
        "ln2_b": nrm(ks[13], (L, D_MODEL), 0.02),
        "w_router": nrm(ks[14], (L, D_MODEL, N_EXPERTS), D_MODEL ** -0.5),
        "w_exp_gate": nrm(ks[15], (L, N_EXPERTS, D_MODEL, EXPERT_FF), D_MODEL ** -0.5),
        "w_exp_up": nrm(ks[16], (L, N_EXPERTS, D_MODEL, EXPERT_FF), D_MODEL ** -0.5),
        "w_exp_down": nrm(ks[17], (L, N_EXPERTS, EXPERT_FF, D_MODEL), EXPERT_FF ** -0.5 * DN_BETA),
        "ln3_g": 1.0 + nrm(ks[18], (L, D_MODEL), 0.02),
        "ln3_b": nrm(ks[19], (L, D_MODEL), 0.02),
    }

def reference(x, mem, w_in, na_rpb, conv_w, w_mix_out, ln1_g, ln1_b,
              w_mem_q, w_mem_k, w_mem_v, w_mem_out, ln2_g, ln2_b,
              w_router, w_exp_gate, w_exp_up, w_exp_down, ln3_g, ln3_b):
    for l in range(DEPTH):
        x = layer_norm(DN_ALPHA * x + hybrid_mixer(x, w_in[l], na_rpb[l], conv_w[l], w_mix_out[l]),
                       ln1_g[l], ln1_b[l])
        x = layer_norm(DN_ALPHA * x + memory_cross_attention(x, mem, w_mem_q[l], w_mem_k[l],
                                                             w_mem_v[l], w_mem_out[l]),
                       ln2_g[l], ln2_b[l])
        x = layer_norm(DN_ALPHA * x + expert_choice_moe(x, w_router[l], w_exp_gate[l],
                                                        w_exp_up[l], w_exp_down[l]),
                       ln3_g[l], ln3_b[l])
    return x


_drawn_inputs = setup_inputs


def setup_inputs(seed=0):
    import zlib

    import numpy as np

    out = dict(_drawn_inputs(seed))
    spreads = {}
    factors = {'na_rpb': 8.0,
     'ln1_b': 2.804,
     'ln3_g': 24.741,
     'ln3_b': 24.153,
     'ln2_g': 2.678,
     'ln2_b': 3.719}
    for name, (base, spread) in spreads.items():
        noise = np.random.default_rng([zlib.crc32(name.encode()), seed]).standard_normal(out[name].shape)
        drawn = base * np.exp(spread * noise) if base else spread * noise
        out[name] = __import__('jax').numpy.asarray(drawn.astype(out[name].dtype))
    for name, factor in factors.items():
        out[name] = (out[name] * factor).astype(out[name].dtype)
    return out
```

```python
from contextlib import ExitStack

import concourse.bass as bass
import numpy as np
from concourse import mybir

F32 = mybir.dt.float32
ALU = mybir.AluOpType
ACT = mybir.ActivationFunctionType
AX = mybir.AxisListType.X

P = 128
D, S, M = 1024, 512, 256
KT, TT, MT = D // P, S // P, M // P
GRID_W, ROWS = 64, S // 64
NAH, NAD = 8, 64
WIN_C = 16
RPB_R, RPB_C = 15, 31
CW = 512
MH = 4
E, CAP, FF = 16, 64, 2048
PAIRS = E // 2
ALPHA = float(2 ** 0.25)
EPS = 1e-5
FMIN = float(np.finfo(np.float32).min)
SLOT = 4096
SLOTS = 8
PSLOTS = 3
CPE = 12
CPP = 2 * CPE
RPB_N = NAH * RPB_R * RPB_C
RPB_PAD = 8
BSEG = 256

C_ID, C_TRI, C_ONE, C_RANK, C_MASK = 0, 128, 256, 384, 448
C_N = C_MASK + 3 * 2 * 16


def shape_constants():
    c = np.zeros((P, C_N), np.float32)
    i = np.arange(P)
    c[:, C_ID:C_ID + P] = i[:, None] == i[None, :]
    c[:, C_TRI:C_TRI + P] = i[:, None] <= i[None, :]
    c[:, C_ONE:C_ONE + P] = 1
    c[:, C_RANK:C_RANK + CAP] = np.arange(1, CAP + 1)
    x = np.arange(16)
    cols = [np.where(x < 8, x, 48 + x)] + [16 * n - 8 + x for n in (1, 2, 3)]
    for kind, g in enumerate((0, 1, 3)):
        col = 16 * g + i % 16
        start = np.clip(col - WIN_C // 2, 0, GRID_W - WIN_C)
        for a in range(2):
            key = cols[(g + a) % 4]
            ok = (key[None, :] >= start[:, None]) & (key[None, :] < start[:, None] + WIN_C)
            c[:, C_MASK + (2 * kind + a) * 16:][:, :16] = np.where(ok, 0, FMIN)
    return c


KIND = (0, 1, 1, 2)
BIAS_AT = ((8, 16), (0, 16), (0, 8))

PJ_C, PJ_H, PJ_B, PJ_MK, PJ_MV, PJ_OUT, PJ_MQ, PJ_MO = 12, 16, 20, 24, 28, 30, 38, 46
TN_MEM, TN_V, TN_NA, TN_X1, TN_MP, TN_X2, TN_AFF, TN_MASK = 8, 12, 16, 32, 40, 48, 56, 57
NU = 16
MU = 8
FILL = [[PJ_C + u] for u in range(4)] + [[PJ_H + u] for u in range(4)] + [[PJ_B + u] for u in range(4)] + \
       [[24, 25], [26, 27], [28], [29]]
CH_MV, CH_OUT, CH_MQ, CH_MO, CHUNKS = 7, 8, 10, 11, 12
CH_DONE = (4, 8, 12, 16, 20, 24, 28, 30, 38, 38, 46, 54)
MIX = 3 + 8


def build(nc, x, mem, w_in, na_rpb, conv_w, w_mix_out, ln1_g, ln1_b, w_mem_q, w_mem_k, w_mem_v, w_mem_out,
          ln2_g, ln2_b, w_router, w_gate, w_up, w_down, ln3_g, ln3_b, consts, out):
    with ExitStack() as ctx:
        def sb(name, *shape):
            return ctx.enter_context(nc.sbuf_tensor(name, [P, *shape], F32))

        def sem(name):
            return ctx.enter_context(nc.semaphore(name))

        ring = sb("ring", SLOTS * SLOT)
        res = sb("res", TT, D)
        xT = sb("xT", KT, S)
        yt = sb("yt", SLOT)
        work = sb("work", 6 * 512)
        kv = sb("kv", 2048)
        ln = sb("ln", 2, D)
        cst = sb("cst", C_N)
        cw = sb("cw", 3, 4)
        wr = sb("wr", KT, E)
        stat = sb("stat", 96)

        na = ring[:, PSLOTS * SLOT:]
        qz = na[:, 0:4096].rearrange("p (h t) -> p h t", h=NAH)
        kT = na[:, 4096:6144].rearrange("p (h t) -> p h t", h=4)
        vp = na[:, 6144:8192].rearrange("p (a n) -> p a n", a=4)
        bias = na[:, 8192:14336].rearrange("p (k h n) -> p k h n", k=3, h=NAH)
        memT = na[:, 14336:16384].rearrange("p (k m) -> p k m", k=KT)
        bT = na[:, 16384:18432].rearrange("p (m t) -> p m t", m=4)
        uT = na[:, 18432:20480].rearrange("p (m t) -> p m t", m=4)
        mem_tok = yt[:, 0:2048].rearrange("p (t d) -> p t d", t=MT)
        rpb_win = yt[:, 2048:4096].rearrange("p (h n) -> p h n", h=NAH)
        yT = yt[:, :].rearrange("p (k t) -> p k t", k=KT)
        cq = yt[:, 0:2048].rearrange("p (h t) -> p h t", h=MH)
        oT = yt[:, 2048:4096].rearrange("p (h t) -> p h t", h=MH)
        sc = [work[:, 512 * b:512 * b + 512].rearrange("p (j n) -> p j n", j=2) for b in range(2)]
        pr = [work[:, 1024 + 512 * b:1536 + 512 * b].rearrange("p (j n) -> p j n", j=2) for b in range(2)]
        prT = [work[:, 2048 + 512 * b:2560 + 512 * b].rearrange("p (j n) -> p j n", j=4) for b in range(2)]
        kmT = kv[:, 0:1024].rearrange("p (h m) -> p h m", h=MH)
        vm = kv[:, 1024:2048].rearrange("p (a n) -> p a n", a=MT)
        ident = cst[:, C_ID:C_ID + P]

        y_acc = xT[:, :, :].rearrange("p k t -> p (k t)").rearrange("p (t d) -> p t d", t=TT)
        xeT = yt[:, 0:1024].rearrange("p (k n) -> p k n", k=KT)
        hidT = yt[:, 1024:1536].rearrange("p (s n) -> p s n", s=4)
        ye = yt[:, 1536:2560]
        scat = yt[:, 2560:3072].rearrange("p (t n) -> p t n", t=TT)
        pick = yt[:, 3072:3584].rearrange("p (t e n) -> p t e n", t=TT, e=2)
        pick_g = yt[:, 3584:4096].rearrange("p (t e n) -> p t e n", t=TT, e=2)
        silu = [work[:, 512 * b:512 * b + 512] for b in range(2)]
        hid = [work[:, 1024 + 512 * b:1536 + 512 * b] for b in range(2)]
        rank = kv[:, 0:64].rearrange("p (i t e) -> p i t e", i=PAIRS, t=TT)
        gate = kv[:, 64:128].rearrange("p (i t e) -> p i t e", i=PAIRS, t=TT)
        aff = kv[:, 128:192].rearrange("p (t e) -> p t e", t=TT)
        mask_tok = kv[:, 192:256].rearrange("p (t e) -> p t e", t=TT)
        afft = kv[0:E, 256:768]
        chosen = kv[0:E, 768:1280]
        top8 = kv[0:E, 1280:1288]

        nmax = [stat[:, 2 * b:2 * b + 2] for b in range(2)]
        ssum = [stat[:, 4 + 2 * b:6 + 2 * b] for b in range(2)]
        rsum = stat[:, 8:10]
        bn = stat[:, 12:24].rearrange("p (a n) -> p a n", a=2)
        mv = stat[:, 24:26]
        var_eps = stat[:, 26:27]
        rstd = stat[:, 27:28]
        neg_half = stat[:, 28:29]
        lmax = stat[:, 32:36]
        lsum = stat[:, 36:40]
        lrec = stat[:, 40:44]

        bank = [ctx.enter_context(nc.psum_tensor(f"bank{n}", [P, 512], F32)) for n in range(8)]
        pj, ps, pt, pv = bank[0:2], bank[2:4], bank[4:6], bank[6:8]

        rpb_pad = nc.dram_tensor("rpb_pad", [RPB_N + 2 * RPB_PAD], F32, kind="Internal").ap()

        x_in = [sem(f"x_in{t}") for t in range(TT)]
        mem_in, cst_in, small_in = sem("mem_in"), sem("cst_in"), sem("small_in")
        rpb_padded, rpb_in = sem("rpb_padded"), sem("rpb_in")
        ln_in = sem("ln_in")
        pre_in = [sem(f"pre_in{s}") for s in range(PSLOTS)]
        exp_in = [sem(f"exp_in{s}") for s in range(SLOTS)]
        exp_used = sem("exp_used")
        turned = sem("turned")
        turn_kept = [sem(f"turn_kept{b}") for b in range(2)]
        projected = sem("projected")
        proj_kept = [sem(f"proj_kept{b}") for b in range(2)]
        scored = sem("scored")
        scores_kept = [sem(f"scores_kept{b}") for b in range(2)]
        pv_done = sem("pv_done")
        att_kept = [sem(f"att_kept{b}") for b in range(2)]
        zeroed, bias_done, maxed, exped, probs_ready, conv_done = (
            sem(n) for n in ("zeroed", "bias_done", "maxed", "exped", "probs_ready", "conv_done"))
        var_ready, rstd_ready, normed = sem("var_ready"), sem("rstd_ready"), sem("normed")
        vec = sem("vec")
        logits_done, lmaxed, lexped, aff_ready, chosen_ready, ranked = (
            sem(n) for n in ("logits_done", "lmaxed", "lexped", "aff_ready", "chosen_ready", "ranked"))
        half_picked, picked, mixed, mix_kept = (sem(n) for n in ("half_picked", "picked", "mixed", "mix_kept"))
        silu_done, hid_ready, hid_turned, hidT_kept, ye_kept = (
            sem(n) for n in ("silu_done", "hid_ready", "hid_turned", "hidT_kept", "ye_kept"))
        stored = sem("stored")

        def cols512(w, n):
            return w.rearrange("(k p) n -> p k n", p=P)[:, :, 512 * n:512 * n + 512]

        win, wmo = w_in[0], w_mix_out[0]
        pre_src = [cols512(win, n) for n in (0, 1, 2, 4, 5, 3)] + \
                  [cols512(w_mem_k[0], 0), cols512(w_mem_v[0], 0), cols512(wmo, 0), cols512(wmo, 1),
                   cols512(w_mem_q[0], 0), w_mem_out[0].rearrange("(k p) n -> p k n", p=P)]

        def pre_chunk(c):
            s = ring[:, (c % PSLOTS) * SLOT:(c % PSLOTS + 1) * SLOT]
            return s.rearrange("p (k n) -> p k n", k=4 if c == CH_MO else KT)

        def exp_chunk(m):
            s = (m + PSLOTS) % SLOTS
            return ring[:, s * SLOT:(s + 1) * SLOT].rearrange("p (k n) -> p k n", k=4)

        wg_v = w_gate[0].rearrange("e (k p) f -> e p k f", p=P)
        wu_v = w_up[0].rearrange("e (k p) f -> e p k f", p=P)
        wd_v = w_down[0].rearrange("e (k p) d -> e p k d", p=P)

        def exp_src(pair, j):
            e, n = 2 * pair + j // CPE, j % CPE
            if n < 8:
                g, w, k = n // 4, (wg_v, wu_v)[n % 4 // 2], 4 * (n % 2)
                return w[bass.ds(e, 1), :, k:k + 4, 1024 * g:1024 * g + 1024].rearrange("e p k f -> (e p) k f")
            k = 4 * (n - 8)
            return wd_v[bass.ds(e, 1), :, k:k + 4, :].rearrange("e p k d -> (e p) k d")

        def key_tokens(v, a):
            if a == 0:
                return v.rearrange("p (r g c) -> p r g c", r=ROWS, g=8)[:, :, 0:8:7, :]
            return v.rearrange("p (r c) -> p r c", r=ROWS)[:, :, 16 * a - 8:16 * a + 8]

        block = ctx.enter_context(nc.Block())

        @block.sync
        def _(sp):
            def load_pre(c):
                if c >= PSLOTS:
                    sp.wait_ge(projected, CH_DONE[c - PSLOTS])
                sp.dma_start(pre_chunk(c), pre_src[c]).then_inc(pre_in[c % PSLOTS], 16)

            def load_exp(m, pair, j):
                sp.dma_start(exp_chunk(m), exp_src(pair, j)).then_inc(exp_in[(m + PSLOTS) % SLOTS], 16)

            for c in range(CH_MO):
                load_pre(c)
            sp.wait_ge(pv_done, NU)
            sp.wait_ge(conv_done, 4)
            sp.wait_ge(projected, CH_DONE[CH_MV])
            for m in range(SLOTS - PSLOTS):
                load_exp(m, 0, m)
            load_pre(CH_MO)
            for m in range(SLOTS - PSLOTS, SLOTS):
                sp.wait_ge(projected, CH_DONE[CHUNKS - SLOTS + m])
                load_exp(m, 0, m)
            with sp.Fori(0, PAIRS - 1) as i:
                for j in range(CPP):
                    m = SLOTS + j
                    sp.wait_ge(exp_used, i * CPP + (j + 1))
                    load_exp(m, i + m // CPP, m % CPP)
            for j in range(CPP - SLOTS):
                sp.wait_ge(exp_used, (PAIRS - 1) * CPP + j + 1)
                load_exp(SLOTS + j, PAIRS - 1, SLOTS + j)

        @block.gpsimd
        def _(pool):
            nc.gpsimd.memset(neg_half, -0.5).then_inc(zeroed, 1)
            nc.gpsimd.memset(qz, 0.0).then_inc(zeroed, 1)
            pool.wait_ge(zeroed, 1)
            for n in range(3 * TT):
                pool.wait_ge(var_ready, n + 1)
                nc.gpsimd.tensor_tensor(rstd, var_eps, neg_half, ALU.pow).then_inc(rstd_ready, 1)

        @block.scalar
        def _(act):
            act.dma_start(cst[:], consts).then_inc(cst_in, 16)
            for t in range(TT):
                act.dma_start(res[:, t, :], x[0, P * t:P * t + P, :]).then_inc(x_in[t], 16)
            act.dma_start(mem_tok, mem[0].rearrange("(t p) d -> p t d", p=P)).then_inc(mem_in, 16)
            flat = na_rpb[0].rearrange("h r c -> (h r c)")
            act.dma_start(rpb_pad[RPB_PAD:RPB_PAD + RPB_N], flat).then_inc(rpb_padded, 16)
            act.dma_start(rpb_pad[0:RPB_PAD], flat[0:RPB_PAD]).then_inc(rpb_padded, 16)
            act.dma_start(rpb_pad[RPB_PAD + RPB_N:], flat[0:RPB_PAD]).then_inc(rpb_padded, 16)
            with nc.allow_non_contiguous_dma(reason="a few per-channel scalars"):
                for k in range(3):
                    act.dma_start(cw[:, k, :], conv_w[0, k].rearrange("(m p) -> p m", p=P)).then_inc(small_in, 16)
            act.dma_start(wr[:], w_router[0].rearrange("(k p) e -> p k e", p=P)).then_inc(small_in, 16)

            def load_ln(g, b):
                act.dma_start(ln[:, 0, :], g.to_broadcast([P, D])).then_inc(ln_in, 16)
                act.dma_start(ln[:, 1, :], b.to_broadcast([P, D])).then_inc(ln_in, 16)

            load_ln(ln1_g, ln1_b)
            act.wait_ge(rpb_padded, 48)
            seg = (ROWS - 1) * RPB_C + 32
            for r in range(ROWS):
                src = bass.AP(rpb_pad.tensor, RPB_C * r, [[1, 16], [RPB_R * RPB_C, NAH], [1, seg]])
                act.dma_start(rpb_win[16 * r:16 * r + 16, :, 0:seg], src).then_inc(rpb_in, 16)

            def keep_turn(n, dst):
                act.wait_ge(turned, n + 1)
                nc.scalar.activation(dst, pt[n % 2][:, :].rearrange("p (a b) -> p a b", a=4), ACT.Copy)\
                    .then_inc(turn_kept[n % 2], 1)

            def keep_proj(n, dst, width=512):
                act.wait_ge(projected, n + 1)
                nc.scalar.activation(dst, pj[n % 2][:, 0:width], ACT.Copy).then_inc(proj_kept[n % 2], 1)

            for n in range(0, 2 * TT, 2):
                keep_turn(n, xT[:, 0:4, P * (n // 2):P * (n // 2) + P])
            act.wait_ge(zeroed, 2)
            for n in range(4):
                act.wait_ge(projected, n + 1)
                for j in range(2):
                    h = slice(64 * j, 64 * j + 64)
                    last = nc.scalar.activation(qz[h, 2 * n + j, :].rearrange("p (g r c) -> p g r c", g=4, r=ROWS),
                                                pj[n % 2][h, :].rearrange("p (r g c) -> p g r c", r=ROWS, g=4),
                                                ACT.Copy, scale=NAD ** -0.5)
                last.then_inc(proj_kept[n % 2], 1)
            for n in range(4, 8):
                keep_proj(n, kT[:, n - 4, :])
            for t in range(MT):
                keep_turn(TN_MEM + 2 * t, memT[:, 0:4, P * t:P * t + P])
            for m in range(4):
                n = 8 + m
                act.wait_ge(projected, n + 1)
                src = pj[n % 2]
                nc.scalar.activation(uT[:, m, 0:P].rearrange("p (r g c) -> p r g c", r=ROWS, g=2),
                                     key_tokens(src[:, :], 0), ACT.Copy)
                nc.scalar.activation(uT[:, m, P:S].rearrange("p (a r x) -> p a r x", a=3, r=ROWS),
                                     src[:, :].rearrange("p (r c) -> p r c", r=ROWS)[:, :, 8:56]
                                     .rearrange("p r (a x) -> p a r x", a=3), ACT.Copy).then_inc(proj_kept[n % 2], 1)
            for m in range(4):
                keep_turn(TN_V + m, vp[:, :, P * m:P * m + P])

            def keep_att(hp):
                act.wait_ge(pv_done, 4 * hp + 4)
                nc.scalar.activation(yT[:, hp, :].rearrange("p (r g c) -> p g r c", r=ROWS, g=4),
                                     pv[hp % 2][:, :].rearrange("p (g r c) -> p g r c", g=4, r=ROWS), ACT.Copy)\
                    .then_inc(att_kept[hp % 2], 1)

            for u in range(NU):
                act.wait_ge(maxed, u + 1)
                if u >= 2:
                    act.wait_ge(turned, TN_NA + u - 1)
                for j in range(2):
                    nc.scalar.activation(pr[u % 2][:, j, :], sc[u % 2][:, j, :], ACT.Exp, bias=nmax[u % 2][:, j:j + 1],
                                         accum_out=ssum[u % 2][:, j:j + 1]).then_inc(exped, 1)
                for n in FILL[u]:
                    if n < PJ_H:
                        keep_proj(n, uT[:, n - PJ_C, :])
                    elif PJ_B <= n < PJ_MK:
                        keep_proj(n, bT[:, n - PJ_B, :])
                    elif PJ_MK <= n < PJ_MV:
                        keep_proj(n, kmT[:, n - PJ_MK, :], M)
                    elif n >= PJ_MV:
                        keep_proj(n, vm[:, n - PJ_MV, :])
                if u >= 2:
                    act.wait_ge(pv_done, u - 1)
                keep_turn(TN_NA + u, prT[u % 2])
                if u % 4 == 0 and u:
                    keep_att(u // 4 - 1)
            keep_att(3)

            def keep_x1(t):
                for a in range(2):
                    keep_turn(TN_X1 + 2 * t + a, xT[:, 4 * a:4 * a + 4, P * t:P * t + P])

            def mem_exp(v):
                b = v % 2
                act.wait_ge(maxed, NU + v + 1)
                act.wait_ge(turned, TN_MP + v - 1 if v >= 2 else TN_NA + NU)
                for j in range(2):
                    nc.scalar.activation(pr[b][:, j, :], ps[b][:, M * j:M * j + M], ACT.Exp,
                                         bias=nmax[b][:, j:j + 1], scale=float(P) ** -0.5,
                                         accum_out=ssum[b][:, j:j + 1]).then_inc(exped, 1)

            def keep_mem(v):
                t, hp = divmod(v, 2)
                act.wait_ge(pv_done, NU + v + 1)
                nc.scalar.activation(oT[:, 2 * hp:2 * hp + 2, P * t:P * t + P],
                                     pv[v % 2][:, 0:256].rearrange("p (j n) -> p j n", j=2), ACT.Copy)\
                    .then_inc(att_kept[v % 2], 1)

            for t in range(3):
                keep_x1(t)
            for h in range(MH):
                keep_proj(PJ_MQ + h, cq[:, h, 0:256], 256)
            mem_exp(0)
            mem_exp(1)
            keep_x1(3)
            for h in range(MH):
                keep_proj(PJ_MQ + 4 + h, cq[:, h, 256:512], 256)
            act.wait_ge(normed, TT)
            load_ln(ln2_g, ln2_b)
            for v in range(MU):
                if v >= 2:
                    act.wait_ge(pv_done, NU + v - 1)
                keep_turn(TN_MP + v, prT[v % 2])
                if v + 2 < MU:
                    mem_exp(v + 2)
                if v:
                    keep_mem(v - 1)
            keep_mem(MU - 1)
            for n in range(2 * TT):
                t, a = divmod(n, 2)
                keep_turn(TN_X2 + n, xT[:, 4 * a:4 * a + 4, P * t:P * t + P])
            act.wait_ge(normed, 2 * TT)
            load_ln(ln3_g, ln3_b)
            act.wait_ge(lmaxed, 1)
            nc.scalar.activation(aff, aff, ACT.Exp).then_inc(lexped, 1)

            with act.Fori(0, PAIRS) as i:
                for e in range(2):
                    for g in range(2):
                        act.wait_ge(exp_used, i * CPP + (CPE * e + 4 * g + 2))
                        nc.scalar.activation(silu[g], bank[2 * g][:, :], ACT.Silu).then_inc(silu_done, 1)
                    for g in range(2):
                        act.wait_ge(hid_turned, i * 4 + (2 * e + g + 1))
                        nc.scalar.activation(hidT, bank[4][:, :].rearrange("p (s n) -> p s n", s=4), ACT.Copy)\
                            .then_inc(hidT_kept, 1)
                    act.wait_ge(exp_used, i * CPP + CPE * (e + 1))
                    for n in range(2):
                        nc.scalar.activation(ye[64 * e:64 * e + 64, 512 * n:512 * n + 512],
                                             bank[5][64 * n:64 * n + 64, :], ACT.Copy).then_inc(ye_kept, 1)
            for t in range(TT):
                act.wait_ge(normed, 2 * TT + t + 1)
                act.dma_start(out[0, P * t:P * t + P, :], y_acc[:, t, :]).then_inc(stored, 16)
            act.wait_ge(stored, 16 * TT)

        @block.tensor
        def _(pe):
            def turn(n, blocks):
                if n >= 2:
                    pe.wait_ge(turn_kept[n % 2], n // 2)
                for a, (src, rows, cols) in enumerate(blocks):
                    mm = nc.tensor.transpose(pt[n % 2][0:cols, a * P:a * P + rows], src, ident[0:rows, 0:rows])
                mm.then_inc(turned, 1)

            def project(n, k, lhs, rhs, width=512):
                if n >= 2:
                    pe.wait_ge(proj_kept[n % 2], n // 2)
                for c in range(k):
                    mm = nc.tensor.matmul(pj[n % 2][:, 0:width], lhs(c), rhs(c), start=c == 0, stop=c == k - 1)
                mm.then_inc(projected, 1)

            def feature_major(n, c, m, rhs, width=512):
                if m == 0:
                    chunk_in(c)
                project(n, KT, lambda k: pre_chunk(c)[:, k, P * m:P * m + P], rhs, width)

            def chunk_in(c):
                pe.wait_ge(pre_in[c % PSLOTS], 16 * (c // PSLOTS + 1))

            def turns_kept(n):
                for b in range(2):
                    pe.wait_ge(turn_kept[b], n // 2 + 1)

            def all_tokens(k):
                return xT[:, k, :]

            pe.wait_ge(cst_in, 16)
            for t in range(TT):
                pe.wait_ge(x_in[t], 16)
                for a in range(2):
                    turn(2 * t + a, [(res[:, t, P * k:P * k + P], P, P) for k in range(4 * a, 4 * a + 4)])
            turns_kept(2 * TT - 1)
            for m in range(4):
                feature_major(m, 0, m, all_tokens)
            for m in range(4):
                feature_major(4 + m, 1, m, all_tokens)
            pe.wait_ge(mem_in, 16)
            for t in range(MT):
                for a in range(2):
                    turn(TN_MEM + 2 * t + a, [(mem_tok[:, t, P * k:P * k + P], P, P) for k in range(4 * a, 4 * a + 4)])

            for m in range(4):
                feature_major(8 + m, 2, m, all_tokens)
            for m in range(4):
                pe.wait_ge(proj_kept[m % 2], (8 + m) // 2 + 1)
                turn(TN_V + m, [(uT[:, m, P * a:P * a + P], P, P) for a in range(4)])

            def filler(n):
                if n < PJ_MK:
                    feature_major(n, 3 + (n - PJ_C) // 4, n % 4, all_tokens)
                    return
                if n == PJ_MK:
                    turns_kept(TN_MEM + 3)
                if n < PJ_MV:
                    feature_major(n, 6, n % 4, lambda k: memT[:, k, :], M)
                    return
                t = n - PJ_MV
                if t == 0:
                    chunk_in(CH_MV)
                project(n, KT, lambda k: memT[:, k, P * t:P * t + P], lambda k: pre_chunk(CH_MV)[:, k, :])

            def na_scores(u):
                hp, g = divmod(u, 4)
                if u == 0:
                    for b in range(2):
                        pe.wait_ge(proj_kept[b], 4)
                if u >= 2:
                    pe.wait_ge(scores_kept[u % 2], u // 2)
                for j in range(2):
                    q = qz[:, 2 * hp + j, P * g:P * g + P]
                    for a in range(2):
                        mm = nc.tensor.matmul(ps[u % 2][:, M * j + P * a:M * j + P * a + P], q,
                                              key_tokens(kT[:, hp, :], (g + a) % 4), start=True, stop=True)
                mm.then_inc(scored, 1)

            def na_pv(u):
                hp, g = divmod(u, 4)
                n = TN_NA + u
                pe.wait_ge(turn_kept[n % 2], n // 2 + 1)
                if u == 0:
                    turns_kept(TN_V + 3)
                if g == 0 and hp >= 2:
                    pe.wait_ge(att_kept[hp % 2], hp // 2)
                for j in range(2):
                    for a in range(2):
                        v = vp[:, (g + a) % 4, NAD * (2 * hp + j):NAD * (2 * hp + j) + NAD]
                        mm = nc.tensor.matmul(pv[hp % 2][64 * j:64 * j + 64, P * g:P * g + P], v,
                                              prT[u % 2][:, 2 * j + a, :], start=a == 0, stop=a == 1)
                mm.then_inc(pv_done, 1)

            def turn_probs(n, b, ready):
                pe.wait_ge(probs_ready, ready)
                turn(n, [(pr[b][:, j, P * a:P * a + P], P, P) for j in range(2) for a in range(2)])

            for u in range(NU):
                na_scores(u)
                for n in FILL[u]:
                    filler(n)
                turn_probs(TN_NA + u, u % 2, u + 1)
                if u:
                    na_pv(u - 1)
            na_pv(NU - 1)

            def mix_out(t):
                for n in range(2):
                    project(PJ_OUT + 2 * t + n, KT, lambda k: yT[:, k, P * t:P * t + P],
                            lambda k: pre_chunk(CH_OUT + n)[:, k, :])

            def turn_res(first, t, done):
                pe.wait_ge(normed, done)
                for a in range(2):
                    turn(first + 2 * t + a, [(res[:, t, P * k:P * k + P], P, P) for k in range(4 * a, 4 * a + 4)])

            def mem_q(half):
                turns_kept(TN_X1 + 4 * half + 3)
                for h in range(MH):
                    w = pre_chunk(CH_MQ)
                    project(PJ_MQ + 4 * half + h, KT, lambda k: w[:, k, P * h:P * h + P],
                            lambda k: xT[:, k, 256 * half:256 * half + 256], 256)

            for b in range(2):
                pe.wait_ge(att_kept[b], 2)
            pe.wait_ge(conv_done, 4)
            chunk_in(CH_OUT)
            chunk_in(CH_OUT + 1)
            mix_out(0)
            mix_out(1)
            turn_res(TN_X1, 0, 1)
            mix_out(2)
            turn_res(TN_X1, 1, 2)
            mix_out(3)
            turn_res(TN_X1, 2, 3)
            chunk_in(CH_MQ)
            mem_q(0)

            def mem_scores(v):
                t, hp = divmod(v, 2)
                n = PJ_MQ + 4 * (t // 2) + 3
                for b in range(2):
                    pe.wait_ge(proj_kept[b], n // 2 + 1)
                if v < 2:
                    pe.wait_ge(scores_kept[v % 2], NU // 2)
                else:
                    pe.wait_ge(exped, 2 * (NU + v - 1))
                for j in range(2):
                    h = 2 * hp + j
                    mm = nc.tensor.matmul(ps[v % 2][:, M * j:M * j + M], cq[:, h, P * t:P * t + P], kmT[:, h, :],
                                          start=True, stop=True)
                mm.then_inc(scored, 1)

            def mem_pv(v):
                t, hp = divmod(v, 2)
                n = TN_MP + v
                pe.wait_ge(turn_kept[n % 2], n // 2 + 1)
                pe.wait_ge(att_kept[v % 2], 2 + v // 2)
                for j in range(2):
                    for a in range(2):
                        mm = nc.tensor.matmul(pv[v % 2][:, P * j:P * j + P], vm[:, a, P * (2 * hp + j):P * (2 * hp + j) + P],
                                              prT[v % 2][:, 2 * j + a, :], start=a == 0, stop=a == 1)
                mm.then_inc(pv_done, 1)

            def mem_out(t):
                for b in range(2):
                    pe.wait_ge(att_kept[b], 2 + t + 1)
                for n in range(2):
                    project(PJ_MO + 2 * t + n, MH, lambda k: oT[:, k, P * t:P * t + P],
                            lambda k: pre_chunk(CH_MO)[:, k, 512 * n:512 * n + 512])

            mem_scores(0)
            mem_scores(1)
            turn_res(TN_X1, 3, 4)
            mem_q(1)
            chunk_in(CH_MO)
            for v in range(MU):
                turn_probs(TN_MP + v, v % 2, NU + v + 1)
                if v + 2 < MU:
                    mem_scores(v + 2)
                if v:
                    mem_pv(v - 1)
                if v in (3, 5, 7):
                    mem_out((v - 3) // 2)
            mem_pv(MU - 1)
            mem_out(3)

            pe.wait_ge(exped, 2 * (NU + MU))
            pe.wait_ge(small_in, 64)
            for t in range(TT):
                turn_res(TN_X2, t, TT + t + 1)
                turns_kept(TN_X2 + 2 * t + 1)
                for k in range(KT):
                    mm = nc.tensor.matmul(ps[0][:, E * t:E * t + E], xT[:, k, P * t:P * t + P], wr[:, k, :],
                                          start=k == 0, stop=k == KT - 1)
            mm.then_inc(logits_done, 1)
            pe.wait_ge(aff_ready, 1)
            turn(TN_AFF, [(aff[:, t, :], P, E) for t in range(TT)])
            pe.wait_ge(chosen_ready, 1)
            turn(TN_MASK, [(chosen[:, P * t:P * t + P], E, P) for t in range(TT)])
            pe.wait_ge(turn_kept[TN_MASK % 2], TN_MASK // 2 + 1)
            for t in range(TT):
                for s in range(t + 1):
                    tri = cst[:, C_TRI:C_TRI + P] if s == t else cst[:, C_ONE:C_ONE + P]
                    mm = nc.tensor.matmul(ps[1][:, E * t:E * t + E], tri, mask_tok[:, s, :], start=s == 0, stop=s == t)
            mm.then_inc(ranked, 1)

            with pe.Fori(0, PAIRS) as i:
                pe.wait_ge(picked, i + 1)
                for a in range(2):
                    if a == 0:
                        pe.wait_ge(mix_kept, i * MIX + 1)
                    for k in range(4):
                        for t in range(TT):
                            mm = nc.tensor.matmul(pv[a][:, P * k:P * k + P],
                                                  res[:, t, P * (4 * a + k):P * (4 * a + k) + P],
                                                  pick[:, t].rearrange("p e n -> p (e n)"), start=t == 0, stop=t == TT - 1)
                    mm.then_inc(mixed, 1)
                pe.wait_ge(mix_kept, i * MIX + 2)
                for t in range(TT):
                    mm = nc.tensor.transpose(pv[0][:, P * t:P * t + P], pick_g[:, t].rearrange("p e n -> p (e n)"), ident)
                mm.then_inc(mixed, 1)
                pe.wait_ge(mix_kept, i * MIX + 3)
                for e in range(2):
                    for g in range(2):
                        pe.wait_ge(hid_ready, i * 4 + (2 * e + g + 1))
                        for n in range(4):
                            j = CPE * e + 4 * g + n
                            expert_in(pe, exp_in, i, j)
                            w = exp_chunk(j)
                            for k in range(4):
                                kk = 4 * (n % 2) + k
                                for c in range(2):
                                    mm = nc.tensor.matmul(bank[2 * g + n // 2][64 * c:64 * c + 64, :],
                                                          xeT[:, kk, 64 * e:64 * e + 64],
                                                          w[:, k, 512 * c:512 * c + 512], start=kk == 0, stop=kk == KT - 1)
                            mm.then_inc(exp_used, 1)
                    if e:
                        pe.wait_ge(ye_kept, i * 4 + 2)
                    for g in range(2):
                        pe.wait_ge(hid_ready, i * 4 + (2 * e + g + 3))
                        for s in range(4):
                            mm = nc.tensor.transpose(bank[4][:, P * s:P * s + P], hid[g][:, P * s:P * s + P], ident)
                        mm.then_inc(hid_turned, 1)
                        pe.wait_ge(hidT_kept, i * 4 + (2 * e + g + 1))
                        for c in range(2):
                            j = CPE * e + 8 + 2 * g + c
                            expert_in(pe, exp_in, i, j)
                            w = exp_chunk(j)
                            for s in range(4):
                                for n in range(2):
                                    mm = nc.tensor.matmul(bank[5][64 * n:64 * n + 64, :], hidT[:, s, 64 * c:64 * c + 64],
                                                          w[:, s, 512 * n:512 * n + 512],
                                                          start=(g, c, s) == (0, 0, 0), stop=(g, c, s) == (1, 1, 3))
                            mm.then_inc(exp_used, 1)
                pe.wait_ge(ye_kept, i * 4 + 4)
                for c in range(2 * TT):
                    t, n = divmod(c, 2)
                    pe.wait_ge(mix_kept, i * MIX + (c + 3 if c else 4))
                    mm = nc.tensor.matmul(pv[(c + 1) % 2][:, :], scat[:, t, :], ye[:, 512 * n:512 * n + 512],
                                          start=True, stop=True)
                    mm.then_inc(mixed, 1)

        @block.vector
        def _(dve):
            links = [0]

            def link(ins):
                links[0] += 1
                ins.then_inc(vec, 1)
                dve.wait_ge(vec, links[0])

            def keep_turn(n, dst):
                dve.wait_ge(turned, n + 1)
                nc.vector.tensor_copy(dst, pt[n % 2][:, :].rearrange("p (a b) -> p a b", a=4))\
                    .then_inc(turn_kept[n % 2], 1)

            for t in range(TT):
                keep_turn(2 * t + 1, xT[:, 4:8, P * t:P * t + P])

            dve.wait_ge(rpb_in, 16 * ROWS)
            dve.wait_ge(cst_in, 16)
            for kind in range(3):
                for a in range(2):
                    win = rpb_win[:, :, (ROWS - 1) * RPB_C + 31 - BIAS_AT[kind][a]:]
                    win = bass.AP(win.tensor, win.offset, [list(win.ap[0]), list(win.ap[1]), [-RPB_C, ROWS], [-1, 16]])
                    m = cst[:, C_MASK + (2 * kind + a) * 16:C_MASK + (2 * kind + a) * 16 + 16]
                    m = bass.AP(m.tensor, m.offset, [list(m.ap[0]), [0, NAH], [0, ROWS], [1, 16]])
                    dst = bias[:, kind, :, P * a:P * a + P].rearrange("p h (r x) -> p h r x", r=ROWS)
                    last = nc.vector.tensor_tensor(dst, win, m, ALU.add)
            last.then_inc(bias_done, 1)
            for t in range(MT):
                keep_turn(TN_MEM + 2 * t + 1, memT[:, 4:8, P * t:P * t + P])
            dve.wait_ge(bias_done, 1)

            def normalise(u):
                b = u % 2
                dve.wait_ge(exped, 2 * (u + 1))
                link(nc.vector.reciprocal(rsum, ssum[b]))
                for j in range(2):
                    last = nc.vector.tensor_scalar(pr[b][:, j, :], pr[b][:, j, :], rsum[:, j:j + 1], None, ALU.mult)
                last.then_inc(probs_ready, 1)

            def conv(m):
                n = PJ_B + m
                dve.wait_ge(proj_kept[n % 2], n // 2 + 1)
                y, u = yT[:, 4 + m, :], uT[:, m, :]
                link(nc.vector.tensor_scalar(y, u, cw[:, 1, m:m + 1], None, ALU.mult))
                link(nc.vector.scalar_tensor_tensor(y[:, 1:S], u[:, 0:S - 1], cw[:, 0, m:m + 1], y[:, 1:S], ALU.mult, ALU.add))
                link(nc.vector.scalar_tensor_tensor(y[:, 0:S - 1], u[:, 1:S], cw[:, 2, m:m + 1], y[:, 0:S - 1], ALU.mult, ALU.add))
                nc.vector.tensor_tensor(y, y, bT[:, m, :], ALU.mult).then_inc(conv_done, 1)

            dve.wait_ge(small_in, 64)
            for u in range(NU):
                hp, g = divmod(u, 4)
                b = u % 2
                dve.wait_ge(scored, u + 1)
                if u >= 2:
                    dve.wait_ge(exped, 2 * (u - 1))
                nc.vector.tensor_tensor(sc[b], ps[b][:, :].rearrange("p (j n) -> p j n", j=2),
                                        bias[:, KIND[g], 2 * hp:2 * hp + 2, :], ALU.add).then_inc(scores_kept[b], 1)
                dve.wait_ge(scores_kept[b], u // 2 + 1)
                nc.vector.tensor_reduce(nmax[b], sc[b], AX, ALU.max, negate=True).then_inc(maxed, 1)
                normalise(u)
                for n in FILL[u]:
                    if PJ_H <= n < PJ_B:
                        dve.wait_ge(projected, n + 1)
                        dve.wait_ge(proj_kept[n % 2], (n - 4) // 2 + 1)
                        nc.vector.tensor_tensor(uT[:, n - PJ_H, :], pj[n % 2][:, :], uT[:, n - PJ_H, :], ALU.mult)\
                            .then_inc(proj_kept[n % 2], 1)
                if 9 <= u < 13:
                    conv(u - 9)

            def norm(buf, t, nth):
                for a in range(2):
                    last = nc.vector.bn_stats(bn[:, a, :], buf[:, t, 512 * a:512 * a + 512])
                link(last)
                link(nc.vector.bn_aggr(mv, bn.rearrange("p a n -> p (a n)")))
                nc.vector.tensor_scalar(var_eps, mv[:, 1:2], EPS, None, ALU.add).then_inc(var_ready, 1)
                dve.wait_ge(rstd_ready, nth + 1)
                dve.wait_ge(ln_in, 32 * (nth // TT + 1))
                link(nc.vector.tensor_scalar(buf[:, t, :], buf[:, t, :], mv[:, 0:1], rstd, ALU.subtract, ALU.mult))
                link(nc.vector.tensor_tensor(buf[:, t, :], buf[:, t, :], ln[:, 0, :], ALU.mult))
                nc.vector.tensor_tensor(buf[:, t, :], buf[:, t, :], ln[:, 1, :], ALU.add).then_inc(normed, 1)

            def add_and_norm(first, t, nth):
                for a in range(2):
                    n = first + 2 * t + a
                    dve.wait_ge(projected, n + 1)
                    r = res[:, t, 512 * a:512 * a + 512]
                    nc.vector.scalar_tensor_tensor(r, r, ALPHA, pj[n % 2][:, :], ALU.mult, ALU.add)\
                        .then_inc(proj_kept[n % 2], 1)
                for a in range(2):
                    n = first + 2 * t + a
                    dve.wait_ge(proj_kept[n % 2], n // 2 + 1)
                norm(res, t, nth)

            for t in range(TT):
                add_and_norm(PJ_OUT, t, t)

            def mem_max(v):
                b = v % 2
                dve.wait_ge(scored, NU + v + 1)
                dve.wait_ge(exped, 2 * (NU + v - 1))
                link(nc.vector.tensor_reduce(nmax[b], ps[b][:, :].rearrange("p (j n) -> p j n", j=2), AX, ALU.max, negate=True))
                nc.vector.tensor_scalar(nmax[b], nmax[b], float(P) ** -0.5, None, ALU.mult).then_inc(maxed, 1)

            mem_max(0)
            mem_max(1)
            for v in range(MU):
                normalise(NU + v)
                if v + 2 < MU:
                    mem_max(v + 2)
                if v in (4, 6):
                    add_and_norm(PJ_MO, (v - 4) // 2, TT + (v - 4) // 2)
            for t in range(2, TT):
                add_and_norm(PJ_MO, t, TT + t)

            lg = ps[0][:, 0:TT * E].rearrange("p (t e) -> p t e", t=TT)

            def per_tile(a):
                return bass.AP(a.tensor, a.offset, [list(a.ap[0]), [1, TT], [0, E]])

            dve.wait_ge(logits_done, 1)
            link(nc.vector.tensor_reduce(lmax, lg, AX, ALU.max))
            nc.vector.tensor_tensor(aff, lg, per_tile(lmax), ALU.subtract).then_inc(lmaxed, 1)
            dve.wait_ge(lexped, 1)
            link(nc.vector.tensor_reduce(lsum, aff, AX, ALU.add))
            link(nc.vector.reciprocal(lrec, lsum))
            nc.vector.tensor_tensor(aff, aff, per_tile(lrec), ALU.mult).then_inc(aff_ready, 1)
            dve.wait_ge(aff_ready, 1)
            nc.vector.tensor_copy(gate.rearrange("p i t e -> p t i e"), aff.rearrange("p t (i e) -> p t i e", e=2))
            dve.wait_ge(turned, TN_AFF + 1)
            nc.vector.tensor_copy(afft, pt[TN_AFF % 2][0:E, :]).then_inc(turn_kept[TN_AFF % 2], 1)
            dve.wait_ge(turn_kept[TN_AFF % 2], TN_AFF // 2 + 1)
            for _ in range(CAP // 8):
                link(nc.vector.max(top8, afft))
                link(nc.vector.match_replace(afft, top8, afft, -1.0))
            nc.vector.tensor_scalar(chosen, afft, 0.0, None, ALU.is_lt).then_inc(chosen_ready, 1)
            dve.wait_ge(turned, TN_MASK + 1)
            nc.vector.tensor_copy(mask_tok, pt[TN_MASK % 2][:, :].rearrange("p (t n) -> p t n", t=TT)[:, :, 0:E])\
                .then_inc(turn_kept[TN_MASK % 2], 1)
            flat_acc = y_acc.rearrange("p t d -> p (t d)")
            flat_res = res[:, :, :].rearrange("p t d -> p (t d)")
            for a, (s, n) in enumerate(((hid_ready, 2), (mix_kept, 1))):
                nc.vector.tensor_scalar(flat_acc[:, 2048 * a:2048 * a + 2048], flat_res[:, 2048 * a:2048 * a + 2048],
                                        ALPHA, None, ALU.mult).then_inc(s, n)
            dve.wait_ge(ranked, 1)
            dve.wait_ge(turn_kept[TN_MASK % 2], TN_MASK // 2 + 1)
            link(nc.vector.tensor_tensor(rank.rearrange("p i t e -> p t i e"),
                                         ps[1][:, 0:TT * E].rearrange("p (t i e) -> p t i e", t=TT, e=2),
                                         mask_tok.rearrange("p t (i e) -> p t i e", e=2), ALU.mult))

            ranks = cst[:, C_RANK:C_RANK + CAP]
            ranks = bass.AP(ranks.tensor, ranks.offset, [list(ranks.ap[0]), [0, 2 * TT], [1, CAP]])

            with dve.Fori(0, PAIRS) as i:
                def by_slot(a):
                    v = a[:, bass.ds(i, 1)]
                    return bass.AP(v.tensor, v.offset, [list(v.ap[0]), [1, 2 * TT], [0, CAP]])

                one = pick.rearrange("p t e n -> p (t e) n")
                one_g = pick_g.rearrange("p t e n -> p (t e) n")
                dve.wait_ge(mix_kept, i * MIX + 1)
                nc.vector.tensor_tensor(one, ranks, by_slot(rank), ALU.is_equal).then_inc(half_picked, 1)
                dve.wait_ge(half_picked, i + 1)
                nc.vector.tensor_tensor(one_g, one, by_slot(gate), ALU.mult).then_inc(picked, 1)
                for a in range(2):
                    dve.wait_ge(mixed, i * MIX + (a + 1))
                    nc.vector.tensor_copy(xeT[:, 4 * a:4 * a + 4, :], pv[a][:, :].rearrange("p (k n) -> p k n", k=4))\
                        .then_inc(mix_kept, 1)
                dve.wait_ge(mixed, i * MIX + 3)
                nc.vector.tensor_copy(scat, pv[0][:, :].rearrange("p (t n) -> p t n", t=TT)).then_inc(mix_kept, 1)
                for e in range(2):
                    for g in range(2):
                        dve.wait_ge(exp_used, i * CPP + (CPE * e + 4 * g + 4))
                        dve.wait_ge(silu_done, i * 4 + (2 * e + g + 1))
                        nc.vector.tensor_tensor(hid[g], bank[2 * g + 1][:, :], silu[g], ALU.mult).then_inc(hid_ready, 1)
                for c in range(2 * TT):
                    t, n = divmod(c, 2)
                    dve.wait_ge(mixed, i * MIX + (c + 4))
                    y = y_acc[:, t, 512 * n:512 * n + 512]
                    nc.vector.tensor_tensor(y, pv[(c + 1) % 2][:, :], y, ALU.add).then_inc(mix_kept, 1)

            dve.wait_ge(mix_kept, PAIRS * MIX + 1)
            for t in range(TT):
                norm(y_acc, t, 2 * TT + t)


def expert_in(pe, exp_in, i, j):
    pe.wait_ge(exp_in[(j + PSLOTS) % SLOTS], i * (16 * CPP // SLOTS) + 16 * (j // SLOTS + 1))


_INS = ["x", "mem", "w_in", "na_rpb", "conv_w", "w_mix_out", "ln1_g", "ln1_b", "w_mem_q", "w_mem_k", "w_mem_v",
        "w_mem_out", "ln2_g", "ln2_b", "w_router", "w_exp_gate", "w_exp_up", "w_exp_down", "ln3_g", "ln3_b"]


def kernel(**inputs):
    import concourse.bacc as bacc
    from concourse.bass_utils import run_bass_kernel_spmd

    nc = bacc.Bacc("TRN2", target_bir_lowering=False, num_devices=1)
    arrays, args = {}, []
    for name in _INS:
        a = inputs[name]
        if name == "na_rpb":
            a = np.flip(np.asarray(a), (2, 3))
        a = np.ascontiguousarray(a)
        arrays[f"in_{name}"] = a
        args.append(nc.dram_tensor(f"in_{name}", a.shape, F32, kind="ExternalInput").ap())
    arrays["shape_consts"] = shape_constants()
    args.append(nc.dram_tensor("shape_consts", [P, C_N], F32, kind="ExternalInput").ap())
    args.append(nc.dram_tensor("out_0", [1, S, D], F32, kind="ExternalOutput").ap())
    build(nc, *args)
    r = run_bass_kernel_spmd(nc, [arrays], core_ids=[0])
    return r.results[0]["out_0"]
```

```python
from contextlib import ExitStack

import concourse.bass as bass
import numpy as np
from concourse import mybir

F32 = mybir.dt.float32
F32R = mybir.dt.float32r
ALU = mybir.AluOpType
ACT = mybir.ActivationFunctionType
AX = mybir.AxisListType.X

P = 128
D, S, M = 1024, 512, 256
KT, TT, MT = D // P, S // P, M // P
GRID_W, ROWS = 64, S // 64
NAH, NAD = 8, 64
WIN_C = 16
RPB_R, RPB_C = 15, 31
CW = 512
MH = 4
E, CAP, FF = 16, 64, 2048
PAIRS = E // 2
ALPHA = float(2 ** 0.25)
EPS = 1e-5
FMIN = float(np.finfo(np.float32).min)
SLOT = 4096
SLOTS = 8
FIRST = 3
CPE = 12
CPP = 2 * CPE
RPB_N = NAH * RPB_R * RPB_C
RPB_PAD = 8
BSEG = 256

C_ID, C_TRI, C_ONE, C_RANK, C_MASK = 0, 128, 256, 384, 448
C_N = C_MASK + 3 * 2 * 16


def shape_constants():
    c = np.zeros((P, C_N), np.float32)
    i = np.arange(P)
    c[:, C_ID:C_ID + P] = i[:, None] == i[None, :]
    c[:, C_TRI:C_TRI + P] = i[:, None] <= i[None, :]
    c[:, C_ONE:C_ONE + P] = 1
    c[:, C_RANK:C_RANK + CAP] = np.arange(1, CAP + 1)
    x = np.arange(16)
    cols = [np.where(x < 8, x, 48 + x)] + [16 * n - 8 + x for n in (1, 2, 3)]
    for kind, g in enumerate((0, 1, 3)):
        col = 16 * g + i % 16
        start = np.clip(col - WIN_C // 2, 0, GRID_W - WIN_C)
        for a in range(2):
            key = cols[(g + a) % 4]
            ok = (key[None, :] >= start[:, None]) & (key[None, :] < start[:, None] + WIN_C)
            c[:, C_MASK + (2 * kind + a) * 16:][:, :16] = np.where(ok, 0, FMIN)
    return c


KIND = (0, 1, 1, 2)
BIAS_AT = ((8, 16), (0, 16), (0, 8))

PJ_MK, PJ_MV, PJ_C, PJ_H, PJ_B, PJ_OUT, PJ_MQ, PJ_MO = 12, 16, 18, 22, 26, 30, 38, 46
TN_MEM, TN_V, TN_NA, TN_X1, TN_MP, TN_X2, TN_AFF, TN_MASK = 8, 12, 16, 32, 40, 48, 56, 57
NU = 16
MU = 8
FILL = [[12, 13], [14, 15], [16], [17]] + [[n] for n in range(PJ_C, PJ_OUT)]
CH_MK, CH_MV, CH_OUT, CH_MQ, CH_MO, CHUNKS = 3, 4, 8, 10, 11, 12
PRE_SLOT = (0, 1, 7, 0, 1, 7, 0, 1, 7, 0, 1, 2)
PIECES = 24
PIECE_CHUNK = [c for c in (0, 1, 2, 5, 6, 7) for _ in range(4)]
PIECE_PJ = list(range(12)) + list(range(PJ_C, PJ_OUT))
MIX = 3 + 8


def build(nc, x, mem, w_in, na_rpb, conv_w, w_mix_out, ln1_g, ln1_b, w_mem_q, w_mem_k, w_mem_v, w_mem_out,
          ln2_g, ln2_b, w_router, w_gate, w_up, w_down, ln3_g, ln3_b, consts, out):
    with ExitStack() as ctx:
        def sb(name, *shape):
            return ctx.enter_context(nc.sbuf_tensor(name, [P, *shape], F32))

        def sem(name):
            return ctx.enter_context(nc.semaphore(name))

        ring = sb("ring", SLOTS * SLOT)
        res = sb("res", TT, D)
        xT = sb("xT", KT, S)
        yt = sb("yt", SLOT)
        work = sb("work", 6 * 512)
        kv = sb("kv", 2048)
        ln = sb("ln", 2, D)
        cst = sb("cst", C_N)
        cw = sb("cw", 3, 4)
        wr = sb("wr", KT, E)
        stat = sb("stat", 96)

        def parts(name, tensor, at, *shape):
            return nc.alloc_sbuf_tensor_at(name, [P, *shape], F32R, offset=nc.lookup_mloc(tensor).addr + 4 * at)

        x_hi = parts("x_hi", xT, 0, KT, S)
        x_lo = parts("x_lo", ring, 3 * SLOT, KT, S)
        piece = parts("piece", ring, 2 * SLOT, 2, 2, KT, P)

        na = ring[:, 4 * SLOT:]
        qz = na[:, 0:4096].rearrange("p (h t) -> p h t", h=NAH)
        kT = na[:, 4096:6144].rearrange("p (h t) -> p h t", h=4)
        vp = na[:, 6144:8192].rearrange("p (a n) -> p a n", a=4)
        memT = na[:, 8192:10240].rearrange("p (k m) -> p k m", k=KT)
        uT = na[:, 10240:12288].rearrange("p (m t) -> p m t", m=4)
        mem_tok = yt[:, 0:2048].rearrange("p (t d) -> p t d", t=MT)
        rpb_win = ln[:, :, :].rearrange("p a d -> p (a d)").rearrange("p (h n) -> p h n", h=NAH)
        yT = yt[:, :].rearrange("p (k t) -> p k t", k=KT)
        cq = yt[:, 0:2048].rearrange("p (h t) -> p h t", h=MH)
        oT = yt[:, 2048:4096].rearrange("p (h t) -> p h t", h=MH)
        sc = [work[:, 512 * b:512 * b + 512].rearrange("p (j n) -> p j n", j=2) for b in range(2)]
        pr = [work[:, 1024 + 512 * b:1536 + 512 * b].rearrange("p (j n) -> p j n", j=2) for b in range(2)]
        prT = [work[:, 2048 + 512 * b:2560 + 512 * b].rearrange("p (j n) -> p j n", j=4) for b in range(2)]
        kmT = kv[:, 0:1024].rearrange("p (h m) -> p h m", h=MH)
        vm = kv[:, 1024:2048].rearrange("p (a n) -> p a n", a=MT)
        ident = cst[:, C_ID:C_ID + P]

        y_acc = xT[:, :, :].rearrange("p k t -> p (k t)").rearrange("p (t d) -> p t d", t=TT)
        xeT = yt[:, 0:1024].rearrange("p (k n) -> p k n", k=KT)
        hidT = yt[:, 1024:1536].rearrange("p (s n) -> p s n", s=4)
        ye = yt[:, 1536:2560]
        scat = yt[:, 2560:3072].rearrange("p (t n) -> p t n", t=TT)
        pick = yt[:, 3072:3584].rearrange("p (t e n) -> p t e n", t=TT, e=2)
        pick_g = yt[:, 3584:4096].rearrange("p (t e n) -> p t e n", t=TT, e=2)
        silu = [work[:, 512 * b:512 * b + 512] for b in range(2)]
        hid = [work[:, 1024 + 512 * b:1536 + 512 * b] for b in range(2)]
        rank = kv[:, 0:64].rearrange("p (i t e) -> p i t e", i=PAIRS, t=TT)
        gate = kv[:, 64:128].rearrange("p (i t e) -> p i t e", i=PAIRS, t=TT)
        aff = kv[:, 128:192].rearrange("p (t e) -> p t e", t=TT)
        mask_tok = kv[:, 192:256].rearrange("p (t e) -> p t e", t=TT)
        afft = kv[0:E, 256:768]
        chosen = kv[0:E, 768:1280]
        top8 = kv[0:E, 1280:1288]

        nmax = [stat[:, 2 * b:2 * b + 2] for b in range(2)]
        ssum = [stat[:, 4 + 2 * b:6 + 2 * b] for b in range(2)]
        rsum = [stat[:, 8 + 2 * b:10 + 2 * b] for b in range(2)]
        bn = stat[:, 12:24].rearrange("p (a n) -> p a n", a=2)
        mv = stat[:, 24:26]
        var_eps = stat[:, 26:27]
        neg_half = stat[:, 28:29]

        def rstd(t):
            return stat[:, 44 + t:45 + t]

        lmax = stat[:, 32:36]
        lsum = stat[:, 36:40]
        lrec = stat[:, 40:44]

        bank = [ctx.enter_context(nc.psum_tensor(f"bank{n}", [P, 512], F32)) for n in range(8)]
        pj, ps, pt, pv = bank[0:2], bank[2:4], bank[4:6], bank[6:8]

        rpb_pad = nc.dram_tensor("rpb_pad", [RPB_N + 2 * RPB_PAD], F32, kind="Internal").ap()

        x_in = [sem(f"x_in{t}") for t in range(TT)]
        q_in = [sem(f"q_in{m}") for m in range(4)]
        ident_in, mem_in, cst_in, small_in = (sem(n) for n in ("ident_in", "mem_in", "cst_in", "small_in"))
        half_set = sem("half_set")
        rpb_padded, rpb_in = sem("rpb_padded"), sem("rpb_in")
        ln_in = sem("ln_in")
        pre_in = {s: sem(f"pre_in{s}") for s in sorted(set(PRE_SLOT))}
        x_hi_kept = sem("x_hi_kept")
        hi_split, lo_split = sem("hi_split"), sem("lo_split")
        exp_in = [sem(f"exp_in{s}") for s in range(SLOTS)]
        exp_used = sem("exp_used")
        turned = sem("turned")
        turn_kept = [sem(f"turn_kept{b}") for b in range(2)]
        projected = sem("projected")
        proj_kept = [sem(f"proj_kept{b}") for b in range(2)]
        scored = sem("scored")
        scores_kept = [sem(f"scores_kept{b}") for b in range(2)]
        pv_done = sem("pv_done")
        att_kept = [sem(f"att_kept{b}") for b in range(2)]
        zeroed, maxed, exped, probs_ready = (sem(n) for n in ("zeroed", "maxed", "exped", "probs_ready"))
        var_ready, gained, rstd_ready, normed, scaled, shifted = (
            sem(n) for n in ("var_ready", "gained", "rstd_ready", "normed", "scaled", "shifted"))
        vec = sem("vec")
        logits_done, lmaxed, lexped, aff_ready, chosen_ready, ranked = (
            sem(n) for n in ("logits_done", "lmaxed", "lexped", "aff_ready", "chosen_ready", "ranked"))
        half_picked, picked, mixed, mix_kept = (sem(n) for n in ("half_picked", "picked", "mixed", "mix_kept"))
        silu_done, hid_ready, hid_turned, hidT_kept, ye_kept = (
            sem(n) for n in ("silu_done", "hid_ready", "hid_turned", "hidT_kept", "ye_kept"))
        stored = sem("stored")

        def cols512(w, n):
            return w.rearrange("(k p) n -> p k n", p=P)[:, :, 512 * n:512 * n + 512]

        win, wmo = w_in[0], w_mix_out[0]
        pre_src = [cols512(win, 0), cols512(win, 1), cols512(win, 2), cols512(w_mem_k[0], 0), cols512(w_mem_v[0], 0),
                   cols512(win, 4), cols512(win, 5), cols512(win, 3), cols512(wmo, 0), cols512(wmo, 1),
                   cols512(w_mem_q[0], 0), w_mem_out[0].rearrange("(k p) n -> p k n", p=P)]

        def pre_chunk(c):
            s = ring[:, PRE_SLOT[c] * SLOT:(PRE_SLOT[c] + 1) * SLOT]
            return s.rearrange("p (k n) -> p k n", k=4 if c == CH_MO else KT)

        def chunk_in(eng, c):
            eng.wait_ge(pre_in[PRE_SLOT[c]], 16 * PRE_SLOT[1:c + 1].count(PRE_SLOT[c]))

        def raw_piece(p):
            return pre_chunk(PIECE_CHUNK[p])[:, :, P * (p % 4):P * (p % 4) + P]

        def exp_chunk(m):
            s = (m + FIRST) % SLOTS
            return ring[:, s * SLOT:(s + 1) * SLOT].rearrange("p (k n) -> p k n", k=4)

        wg_v = w_gate[0].rearrange("e (k p) f -> e p k f", p=P)
        wu_v = w_up[0].rearrange("e (k p) f -> e p k f", p=P)
        wd_v = w_down[0].rearrange("e (k p) d -> e p k d", p=P)

        def exp_src(pair, j):
            e, n = 2 * pair + j // CPE, j % CPE
            if n < 8:
                g, w, k = n // 4, (wg_v, wu_v)[n % 4 // 2], 4 * (n % 2)
                return w[bass.ds(e, 1), :, k:k + 4, 1024 * g:1024 * g + 1024].rearrange("e p k f -> (e p) k f")
            k = 4 * (n - 8)
            return wd_v[bass.ds(e, 1), :, k:k + 4, :].rearrange("e p k d -> (e p) k d")

        def key_tokens(v, a):
            if a == 0:
                return v.rearrange("p (r g c) -> p r g c", r=ROWS, g=8)[:, :, 0:8:7, :]
            return v.rearrange("p (r c) -> p r c", r=ROWS)[:, :, 16 * a - 8:16 * a + 8]

        block = ctx.enter_context(nc.Block())

        @block.sync
        def _(sp):
            def load_pre(c):
                sp.dma_start(pre_chunk(c), pre_src[c]).then_inc(pre_in[PRE_SLOT[c]], 16)

            def load_exp(m, pair, j):
                sp.dma_start(exp_chunk(m), exp_src(pair, j)).then_inc(exp_in[(m + FIRST) % SLOTS], 16)

            sp.dma_start(cst[:, 0:C_TRI], consts[:, 0:C_TRI]).then_inc(ident_in, 16)
            for t in range(TT):
                sp.dma_start(res[:, t, :], x[0, P * t:P * t + P, :]).then_inc(x_in[t], 16)
            for m in range(4):
                sp.dma_start(raw_piece(m), pre_src[0][:, :, P * m:P * m + P]).then_inc(q_in[m], 16)
            load_pre(1)
            load_pre(2)
            sp.wait_ge(lo_split, 4)
            load_pre(CH_MK)
            sp.wait_ge(lo_split, 8)
            load_pre(CH_MV)
            sp.wait_ge(lo_split, 12)
            load_pre(5)
            sp.wait_ge(projected, PJ_MV)
            load_pre(6)
            sp.wait_ge(projected, PJ_C)
            load_pre(7)
            for c, done in ((CH_OUT, 16), (CH_OUT + 1, 20), (CH_MQ, 24)):
                sp.wait_ge(lo_split, done)
                load_pre(c)
            sp.wait_ge(projected, PJ_OUT)
            load_pre(CH_MO)
            load_exp(0, 0, 0)
            sp.wait_ge(pv_done, NU)
            for b in range(2):
                sp.wait_ge(proj_kept[b], PJ_OUT // 2)
            for m in range(1, 4):
                load_exp(m, 0, m)
            for m, done in ((4, PJ_MQ), (5, PJ_MQ), (6, PJ_MO), (7, PJ_MO + 8)):
                sp.wait_ge(projected, done)
                load_exp(m, 0, m)
            with sp.Fori(0, PAIRS - 1) as i:
                for j in range(CPP):
                    m = SLOTS + j
                    sp.wait_ge(exp_used, i * CPP + (j + 1))
                    load_exp(m, i + m // CPP, m % CPP)
            for j in range(CPP - SLOTS):
                sp.wait_ge(exp_used, (PAIRS - 1) * CPP + j + 1)
                load_exp(SLOTS + j, PAIRS - 1, SLOTS + j)
            for t in range(TT):
                if t < TT - 1:
                    sp.wait_ge(shifted, t + 1)
                else:
                    sp.wait_ge(normed, 2 * TT + 1)
                sp.dma_start(out[0, P * t:P * t + P, :], y_acc[:, t, :]).then_inc(stored, 16)
            sp.wait_ge(stored, 16 * TT)

        @block.gpsimd
        def _(pool):
            nc.gpsimd.memset(neg_half, -0.5).then_inc(half_set, 1)
            for p in range(PIECES):
                pool.wait_ge(hi_split, p + 1)
                nc.gpsimd.tensor_tensor(piece[:, p % 2, 1, :, :], raw_piece(p), piece[:, p % 2, 0, :, :].bitcast(F32),
                                        ALU.subtract).then_inc(lo_split, 1)
            pool.wait_ge(half_set, 1)
            def inverse_std(n):
                pool.wait_ge(var_ready, n + 1)
                nc.gpsimd.tensor_tensor(rstd(n % TT), var_eps, neg_half, ALU.pow).then_inc(rstd_ready, 1)

            def add_b(t):
                pool.wait_ge(scaled, t + 1)
                y = y_acc[:, t, :]
                nc.gpsimd.tensor_tensor(y, y, ln[:, 1, :], ALU.add).then_inc(shifted, 1)

            for n in range(3 * TT):
                inverse_std(n)
                if n > 2 * TT:
                    add_b(n - 2 * TT - 1)

        @block.scalar
        def _(act):
            def load_ln(g, b):
                act.dma_start(ln[:, 0, :], g.to_broadcast([P, D])).then_inc(ln_in, 16)
                act.dma_start(ln[:, 1, :], b.to_broadcast([P, D])).then_inc(ln_in, 16)

            def load_small():
                act.dma_start(mem_tok, mem[0].rearrange("(t p) d -> p t d", p=P)).then_inc(mem_in, 16)
                act.dma_start(cst[:, C_TRI:], consts[:, C_TRI:]).then_inc(cst_in, 16)
                flat = na_rpb[0].rearrange("h r c -> (h r c)")
                act.dma_start(rpb_pad[RPB_PAD:RPB_PAD + RPB_N], flat).then_inc(rpb_padded, 16)
                act.dma_start(rpb_pad[0:RPB_PAD], flat[0:RPB_PAD]).then_inc(rpb_padded, 16)
                act.dma_start(rpb_pad[RPB_PAD + RPB_N:], flat[0:RPB_PAD]).then_inc(rpb_padded, 16)
                with nc.allow_non_contiguous_dma(reason="a few per-channel scalars"):
                    for k in range(3):
                        act.dma_start(cw[:, k, :], conv_w[0, k].rearrange("(m p) -> p m", p=P)).then_inc(small_in, 16)
                act.dma_start(wr[:], w_router[0].rearrange("(k p) e -> p k e", p=P)).then_inc(small_in, 16)

            seg = (ROWS - 1) * RPB_C + 32
            def load_bias():
                act.wait_ge(rpb_padded, 48)
                for r in range(ROWS):
                    src = bass.AP(rpb_pad.tensor, RPB_C * r, [[1, 16], [RPB_R * RPB_C, NAH], [1, seg]])
                    act.dma_start(rpb_win[16 * r:16 * r + 16, :, 0:seg], src).then_inc(rpb_in, 16)

            def split(p):
                if p < 4:
                    act.wait_ge(q_in[p], 16)
                else:
                    chunk_in(act, PIECE_CHUNK[p])
                if p >= 2:
                    act.wait_ge(projected, PIECE_PJ[p - 2] + 1)
                nc.scalar.activation(piece[:, p % 2, 0, :, :], raw_piece(p), ACT.Copy).then_inc(hi_split, 1)

            def keep_turn(n, dst):
                act.wait_ge(turned, n + 1)
                nc.scalar.activation(dst, pt[n % 2][:, :].rearrange("p (a b) -> p a b", a=4), ACT.Copy)\
                    .then_inc(turn_kept[n % 2], 1)

            def keep_proj(n, dst, width=512):
                act.wait_ge(projected, n + 1)
                nc.scalar.activation(dst, pj[n % 2][:, 0:width], ACT.Copy).then_inc(proj_kept[n % 2], 1)

            for n in range(2 * TT):
                t, a = divmod(n, 2)
                act.wait_ge(turned, n + 1)
                nc.scalar.activation(x_hi[:, 4 * a:4 * a + 4, P * t:P * t + P],
                                     pt[n % 2][:, :].rearrange("p (a b) -> p a b", a=4), ACT.Copy).then_inc(x_hi_kept, 1)
            split(0)
            split(1)
            load_small()
            for n in range(4):
                split(n + 2)
                if n == 0:
                    act.wait_ge(zeroed, 1)
                act.wait_ge(projected, n + 1)
                for j in range(2):
                    h = slice(64 * j, 64 * j + 64)
                    last = nc.scalar.activation(qz[h, 2 * n + j, :].rearrange("p (g r c) -> p g r c", g=4, r=ROWS),
                                                pj[n % 2][h, :].rearrange("p (r g c) -> p g r c", r=ROWS, g=4),
                                                ACT.Copy, scale=NAD ** -0.5)
                last.then_inc(proj_kept[n % 2], 1)
            load_bias()
            for n in range(4, 8):
                split(n + 2)
                keep_proj(n, kT[:, n - 4, :])
            for t in range(MT):
                keep_turn(TN_MEM + 2 * t, memT[:, 0:4, P * t:P * t + P])
            for m in range(4):
                n = 8 + m
                if m < 2:
                    split(n + 2)
                act.wait_ge(projected, n + 1)
                src = pj[n % 2]
                nc.scalar.activation(uT[:, m, 0:P].rearrange("p (r g c) -> p r g c", r=ROWS, g=2),
                                     key_tokens(src[:, :], 0), ACT.Copy)
                nc.scalar.activation(uT[:, m, P:S].rearrange("p (a r x) -> p a r x", a=3, r=ROWS),
                                     src[:, :].rearrange("p (r c) -> p r c", r=ROWS)[:, :, 8:56]
                                     .rearrange("p r (a x) -> p a r x", a=3), ACT.Copy).then_inc(proj_kept[n % 2], 1)
            for m in range(4):
                keep_turn(TN_V + m, vp[:, :, P * m:P * m + P])

            def keep_att(hp):
                act.wait_ge(pv_done, 4 * hp + 4)
                nc.scalar.activation(yT[:, hp, :].rearrange("p (r g c) -> p g r c", r=ROWS, g=4),
                                     pv[hp % 2][:, :].rearrange("p (g r c) -> p g r c", g=4, r=ROWS), ACT.Copy)\
                    .then_inc(att_kept[hp % 2], 1)

            for u in range(NU):
                act.wait_ge(maxed, u + 1)
                if u >= 2:
                    act.wait_ge(turned, TN_NA + u - 1)
                for j in range(2):
                    nc.scalar.activation(pr[u % 2][:, j, :], sc[u % 2][:, j, :], ACT.Exp, bias=nmax[u % 2][:, j:j + 1],
                                         accum_out=ssum[u % 2][:, j:j + 1]).then_inc(exped, 1)
                if 4 <= u < NU - 2:
                    split(10 + u)
                for n in FILL[u]:
                    if n < PJ_MV:
                        keep_proj(n, kmT[:, n - PJ_MK, :], M)
                    elif n < PJ_C:
                        keep_proj(n, vm[:, n - PJ_MV, :])
                    elif n < PJ_H:
                        keep_proj(n, uT[:, n - PJ_C, :])
                if u >= 2:
                    act.wait_ge(pv_done, u - 1)
                keep_turn(TN_NA + u, prT[u % 2])
                if u in (1, 2):
                    split(11 + u)
                if u % 4 == 0 and u:
                    keep_att(u // 4 - 1)
            load_ln(ln1_g, ln1_b)
            keep_att(3)

            def keep_x1(t):
                for a in range(2):
                    keep_turn(TN_X1 + 2 * t + a, xT[:, 4 * a:4 * a + 4, P * t:P * t + P])

            def mem_exp(v):
                b = v % 2
                act.wait_ge(maxed, NU + v + 1)
                act.wait_ge(turned, TN_MP + v - 1 if v >= 2 else TN_NA + NU)
                for j in range(2):
                    nc.scalar.activation(pr[b][:, j, :], ps[b][:, M * j:M * j + M], ACT.Exp,
                                         bias=nmax[b][:, j:j + 1], scale=float(P) ** -0.5,
                                         accum_out=ssum[b][:, j:j + 1]).then_inc(exped, 1)

            def keep_mem(v):
                t, hp = divmod(v, 2)
                act.wait_ge(pv_done, NU + v + 1)
                nc.scalar.activation(oT[:, 2 * hp:2 * hp + 2, P * t:P * t + P],
                                     pv[v % 2][:, 0:256].rearrange("p (j n) -> p j n", j=2), ACT.Copy)\
                    .then_inc(att_kept[v % 2], 1)

            for t in range(3):
                keep_x1(t)
            for h in range(MH):
                keep_proj(PJ_MQ + h, cq[:, h, 0:256], 256)
            keep_x1(3)
            mem_exp(0)
            mem_exp(1)
            for h in range(MH):
                keep_proj(PJ_MQ + 4 + h, cq[:, h, 256:512], 256)
            act.wait_ge(normed, TT)
            load_ln(ln2_g, ln2_b)
            for v in range(MU):
                if v >= 2:
                    act.wait_ge(pv_done, NU + v - 1)
                keep_turn(TN_MP + v, prT[v % 2])
                if v + 2 < MU:
                    mem_exp(v + 2)
                if v:
                    keep_mem(v - 1)
            keep_mem(MU - 1)
            for n in range(2 * TT - 1):
                t, a = divmod(n, 2)
                keep_turn(TN_X2 + n, xT[:, 4 * a:4 * a + 4, P * t:P * t + P])
            act.wait_ge(normed, 2 * TT)
            load_ln(ln3_g, ln3_b)
            act.wait_ge(lmaxed, 1)
            nc.scalar.activation(aff, aff, ACT.Exp).then_inc(lexped, 1)

            with act.Fori(0, PAIRS) as i:
                for e in range(2):
                    for g in range(2):
                        act.wait_ge(exp_used, i * CPP + (CPE * e + 4 * g + 2))
                        nc.scalar.activation(silu[g], bank[2 * g][:, :], ACT.Silu).then_inc(silu_done, 1)
                    for g in range(2):
                        act.wait_ge(hid_turned, i * 4 + (2 * e + g + 1))
                        nc.scalar.activation(hidT, bank[4][:, :].rearrange("p (s n) -> p s n", s=4), ACT.Copy)\
                            .then_inc(hidT_kept, 1)
                    act.wait_ge(exp_used, i * CPP + CPE * (e + 1))
                    for n in range(2):
                        nc.scalar.activation(ye[64 * e:64 * e + 64, 512 * n:512 * n + 512],
                                             bank[5][64 * n:64 * n + 64, :], ACT.Copy).then_inc(ye_kept, 1)
            for t in range(TT - 1):
                act.wait_ge(gained, 2 * TT + t + 1)
                act.wait_ge(rstd_ready, 2 * TT + t + 1)
                nc.scalar.activation(y_acc[:, t, :], y_acc[:, t, :], ACT.Copy, scale=rstd(t)).then_inc(scaled, 1)

        @block.tensor
        def _(pe):
            def turn(n, blocks):
                if n >= 2:
                    pe.wait_ge(turn_kept[n % 2], n // 2)
                for a, (src, rows, cols) in enumerate(blocks):
                    mm = nc.tensor.transpose(pt[n % 2][0:cols, a * P:a * P + rows], src, ident[0:rows, 0:rows])
                mm.then_inc(turned, 1)

            def project(n, k, lhs, rhs, width=512, before_last=()):
                if n >= 2:
                    pe.wait_ge(proj_kept[n % 2], n // 2)
                for c in range(k):
                    if c == k - 1:
                        for semaphore, value in before_last:
                            pe.wait_ge(semaphore, value)
                    mm = nc.tensor.matmul(pj[n % 2][:, 0:width], lhs(c), rhs(c), start=c == 0, stop=c == k - 1)
                mm.then_inc(projected, 1)

            def from_x(p):
                n = PIECE_PJ[p]
                hi, lo = piece[:, p % 2, 0], piece[:, p % 2, 1]
                if n >= 2:
                    pe.wait_ge(proj_kept[n % 2], n // 2)
                pe.wait_ge(hi_split, p + 1)
                for k in range(KT):
                    nc.tensor.matmul(pj[n % 2][:, :], hi[:, k, :], x_hi[:, k, :], start=k == 0, stop=False)
                for k in range(KT):
                    nc.tensor.matmul(pj[n % 2][:, :], hi[:, k, :], x_lo[:, k, :], start=False, stop=False)
                pe.wait_ge(lo_split, p + 1)
                for k in range(KT):
                    mm = nc.tensor.matmul(pj[n % 2][:, :], lo[:, k, :], x_hi[:, k, :], start=False, stop=k == KT - 1)
                mm.then_inc(projected, 1)

            def turns_kept(n):
                for b in range(2):
                    pe.wait_ge(turn_kept[b], n // 2 + 1)

            pe.wait_ge(ident_in, 16)
            for t in range(TT):
                pe.wait_ge(x_in[t], 16)
                for a in range(2):
                    turn(2 * t + a, [(res[:, t, P * k:P * k + P], P, P) for k in range(4 * a, 4 * a + 4)])
            turns_kept(2 * TT - 1)
            for p in range(8):
                from_x(p)
            pe.wait_ge(mem_in, 16)
            for t in range(MT):
                for a in range(2):
                    turn(TN_MEM + 2 * t + a, [(mem_tok[:, t, P * k:P * k + P], P, P) for k in range(4 * a, 4 * a + 4)])
            for p in range(8, 12):
                from_x(p)
            for m in range(4):
                pe.wait_ge(proj_kept[m % 2], (8 + m) // 2 + 1)
                turn(TN_V + m, [(uT[:, m, P * a:P * a + P], P, P) for a in range(4)])

            def filler(n):
                if n >= PJ_C:
                    from_x(12 + n - PJ_C)
                elif n < PJ_MV:
                    m = n - PJ_MK
                    if m == 0:
                        turns_kept(TN_MEM + 3)
                        chunk_in(pe, CH_MK)
                    project(n, KT, lambda k: pre_chunk(CH_MK)[:, k, P * m:P * m + P], lambda k: memT[:, k, :], M)
                else:
                    t = n - PJ_MV
                    if t == 0:
                        chunk_in(pe, CH_MV)
                    project(n, KT, lambda k: memT[:, k, P * t:P * t + P], lambda k: pre_chunk(CH_MV)[:, k, :])

            def na_scores(u):
                hp, g = divmod(u, 4)
                if u == 0:
                    for b in range(2):
                        pe.wait_ge(proj_kept[b], 4)
                if u >= 2:
                    pe.wait_ge(scores_kept[u % 2], u // 2)
                for j in range(2):
                    q = qz[:, 2 * hp + j, P * g:P * g + P]
                    for a in range(2):
                        mm = nc.tensor.matmul(ps[u % 2][:, M * j + P * a:M * j + P * a + P], q,
                                              key_tokens(kT[:, hp, :], (g + a) % 4), start=True, stop=True)
                mm.then_inc(scored, 1)

            def na_pv(u):
                hp, g = divmod(u, 4)
                n = TN_NA + u
                pe.wait_ge(turn_kept[n % 2], n // 2 + 1)
                if u == 0:
                    turns_kept(TN_V + 3)
                if g == 0 and hp >= 2:
                    pe.wait_ge(att_kept[hp % 2], hp // 2)
                for j in range(2):
                    for a in range(2):
                        v = vp[:, (g + a) % 4, NAD * (2 * hp + j):NAD * (2 * hp + j) + NAD]
                        mm = nc.tensor.matmul(pv[hp % 2][64 * j:64 * j + 64, P * g:P * g + P], v,
                                              prT[u % 2][:, 2 * j + a, :], start=a == 0, stop=a == 1)
                mm.then_inc(pv_done, 1)

            def turn_probs(n, b, ready):
                pe.wait_ge(probs_ready, ready)
                turn(n, [(pr[b][:, j, P * a:P * a + P], P, P) for j in range(2) for a in range(2)])

            for u in range(NU):
                na_scores(u)
                for n in FILL[u]:
                    filler(n)
                turn_probs(TN_NA + u, u % 2, u + 1)
                if u:
                    na_pv(u - 1)
            na_pv(NU - 1)

            def mix_out(t):
                for n in range(2):
                    project(PJ_OUT + 2 * t + n, KT, lambda k: yT[:, (k + 4) % KT, P * t:P * t + P],
                            lambda k: pre_chunk(CH_OUT + n)[:, (k + 4) % KT, :], before_last=[(att_kept[1], 2)])

            def turn_res(first, t, done):
                pe.wait_ge(normed, done)
                for a in range(2):
                    turn(first + 2 * t + a, [(res[:, t, P * k:P * k + P], P, P) for k in range(4 * a, 4 * a + 4)])

            def mem_q(half):
                turns_kept(TN_X1 + 4 * half + 3)
                for h in range(MH):
                    w = pre_chunk(CH_MQ)
                    project(PJ_MQ + 4 * half + h, KT, lambda k: w[:, k, P * h:P * h + P],
                            lambda k: xT[:, k, 256 * half:256 * half + 256], 256)

            pe.wait_ge(att_kept[0], 2)
            pe.wait_ge(att_kept[1], 1)
            for b in range(2):
                pe.wait_ge(proj_kept[b], PJ_OUT // 2)
            chunk_in(pe, CH_OUT)
            chunk_in(pe, CH_OUT + 1)
            mix_out(0)
            mix_out(1)
            turn_res(TN_X1, 0, 1)
            mix_out(2)
            turn_res(TN_X1, 1, 2)
            mix_out(3)
            turn_res(TN_X1, 2, 3)
            chunk_in(pe, CH_MQ)
            mem_q(0)

            def mem_scores(v):
                t, hp = divmod(v, 2)
                n = PJ_MQ + 4 * (t // 2) + 3
                for b in range(2):
                    pe.wait_ge(proj_kept[b], n // 2 + 1)
                if v < 2:
                    pe.wait_ge(scores_kept[v % 2], NU // 2)
                else:
                    pe.wait_ge(exped, 2 * (NU + v - 1))
                for j in range(2):
                    h = 2 * hp + j
                    mm = nc.tensor.matmul(ps[v % 2][:, M * j:M * j + M], cq[:, h, P * t:P * t + P], kmT[:, h, :],
                                          start=True, stop=True)
                mm.then_inc(scored, 1)

            def mem_pv(v):
                t, hp = divmod(v, 2)
                n = TN_MP + v
                pe.wait_ge(turn_kept[n % 2], n // 2 + 1)
                pe.wait_ge(att_kept[v % 2], 2 + v // 2)
                for j in range(2):
                    for a in range(2):
                        mm = nc.tensor.matmul(pv[v % 2][:, P * j:P * j + P], vm[:, a, P * (2 * hp + j):P * (2 * hp + j) + P],
                                              prT[v % 2][:, 2 * j + a, :], start=a == 0, stop=a == 1)
                mm.then_inc(pv_done, 1)

            def mem_out(t):
                for b in range(2):
                    pe.wait_ge(att_kept[b], 2 + t + 1)
                for n in range(2):
                    project(PJ_MO + 2 * t + n, MH, lambda k: oT[:, k, P * t:P * t + P],
                            lambda k: pre_chunk(CH_MO)[:, k, 512 * n:512 * n + 512])

            turn_res(TN_X1, 3, 4)
            mem_scores(0)
            mem_scores(1)
            mem_q(1)
            chunk_in(pe, CH_MO)
            for v in range(MU):
                turn_probs(TN_MP + v, v % 2, NU + v + 1)
                if v + 2 < MU:
                    mem_scores(v + 2)
                if v:
                    mem_pv(v - 1)
                if v in (3, 5, 7):
                    mem_out((v - 3) // 2)
            mem_pv(MU - 1)
            mem_out(3)

            pe.wait_ge(exped, 2 * (NU + MU))
            pe.wait_ge(small_in, 64)
            pe.wait_ge(cst_in, 16)
            turn_res(TN_X2, 0, TT + 1)
            for t in range(TT):
                if t + 1 < TT:
                    turn_res(TN_X2, t + 1, TT + t + 2)
                turns_kept(TN_X2 + 2 * t + 1)
                for k in range(KT):
                    mm = nc.tensor.matmul(ps[0][:, E * t:E * t + E], xT[:, k, P * t:P * t + P], wr[:, k, :],
                                          start=k == 0, stop=k == KT - 1)
            mm.then_inc(logits_done, 1)
            pe.wait_ge(aff_ready, 1)
            turn(TN_AFF, [(aff[:, t, :], P, E) for t in range(TT)])
            pe.wait_ge(chosen_ready, 1)
            turn(TN_MASK, [(chosen[:, P * t:P * t + P], E, P) for t in range(TT)])
            pe.wait_ge(turn_kept[TN_MASK % 2], TN_MASK // 2 + 1)
            flat_mask = mask_tok.rearrange("p t e -> p (t e)")
            for back in range(TT):
                lhs = cst[:, C_ONE:C_ONE + P] if back else cst[:, C_TRI:C_TRI + P]
                mm = nc.tensor.matmul(ps[1][:, E * back:TT * E], lhs, flat_mask[:, 0:(TT - back) * E],
                                      start=back == 0, stop=back == TT - 1)
            mm.then_inc(ranked, 1)

            with pe.Fori(0, PAIRS) as i:
                pe.wait_ge(half_picked, i + 1)
                for a in range(2):
                    if a == 0:
                        pe.wait_ge(mix_kept, i * MIX + 1)
                    for k in range(4):
                        for t in range(TT):
                            mm = nc.tensor.matmul(pv[a][:, P * k:P * k + P],
                                                  res[:, t, P * (4 * a + k):P * (4 * a + k) + P],
                                                  pick[:, t].rearrange("p e n -> p (e n)"), start=t == 0, stop=t == TT - 1)
                    mm.then_inc(mixed, 1)
                pe.wait_ge(mix_kept, i * MIX + 3)
                for e in range(2):
                    if e:
                        pe.wait_ge(picked, i + 1)
                        for t in range(TT):
                            mm = nc.tensor.transpose(pv[0][:, P * t:P * t + P], pick_g[:, t].rearrange("p e n -> p (e n)"),
                                                     ident)
                        mm.then_inc(mixed, 1)
                    for g in range(2):
                        pe.wait_ge(hid_ready, i * 4 + (2 * e + g + 1))
                        for n in range(4):
                            j = CPE * e + 4 * g + n
                            expert_in(pe, exp_in, i, j)
                            w = exp_chunk(j)
                            for k in range(4):
                                kk = 4 * (n % 2) + k
                                for c in range(2):
                                    mm = nc.tensor.matmul(bank[2 * g + n // 2][64 * c:64 * c + 64, :],
                                                          xeT[:, kk, 64 * e:64 * e + 64],
                                                          w[:, k, 512 * c:512 * c + 512], start=kk == 0, stop=kk == KT - 1)
                            mm.then_inc(exp_used, 1)
                    if e:
                        pe.wait_ge(ye_kept, i * 4 + 2)
                    for g in range(2):
                        pe.wait_ge(hid_ready, i * 4 + (2 * e + g + 3))
                        for s in range(4):
                            mm = nc.tensor.transpose(bank[4][:, P * s:P * s + P], hid[g][:, P * s:P * s + P], ident)
                        mm.then_inc(hid_turned, 1)
                        pe.wait_ge(hidT_kept, i * 4 + (2 * e + g + 1))
                        for c in range(2):
                            j = CPE * e + 8 + 2 * g + c
                            expert_in(pe, exp_in, i, j)
                            w = exp_chunk(j)
                            for s in range(4):
                                for n in range(2):
                                    mm = nc.tensor.matmul(bank[5][64 * n:64 * n + 64, :], hidT[:, s, 64 * c:64 * c + 64],
                                                          w[:, s, 512 * n:512 * n + 512],
                                                          start=(g, c, s) == (0, 0, 0), stop=(g, c, s) == (1, 1, 3))
                            mm.then_inc(exp_used, 1)
                pe.wait_ge(ye_kept, i * 4 + 4)
                for c in range(2 * TT):
                    t, n = divmod(c, 2)
                    pe.wait_ge(mix_kept, i * MIX + (c + 3 if c else 4))
                    mm = nc.tensor.matmul(pv[(c + 1) % 2][:, :], scat[:, t, :], ye[:, 512 * n:512 * n + 512],
                                          start=True, stop=True)
                    mm.then_inc(mixed, 1)

        @block.vector
        def _(dve):
            links = [0]

            def link(ins):
                links[0] += 1
                ins.then_inc(vec, 1)
                dve.wait_ge(vec, links[0])

            def keep_turn(n, dst):
                dve.wait_ge(turned, n + 1)
                nc.vector.tensor_copy(dst, pt[n % 2][:, :].rearrange("p (a b) -> p a b", a=4))\
                    .then_inc(turn_kept[n % 2], 1)

            nc.vector.memset(qz, 0.0).then_inc(zeroed, 1)
            for n in range(2 * TT):
                t, a = divmod(n, 2)
                hi = x_hi[:, 4 * a:4 * a + 4, P * t:P * t + P].bitcast(F32)
                dve.wait_ge(x_hi_kept, n + 1)
                nc.vector.tensor_tensor(x_lo[:, 4 * a:4 * a + 4, P * t:P * t + P],
                                        pt[n % 2][:, :].rearrange("p (a b) -> p a b", a=4), hi, ALU.subtract)\
                    .then_inc(turn_kept[n % 2], 1)
            for t in range(MT):
                keep_turn(TN_MEM + 2 * t + 1, memT[:, 4:8, P * t:P * t + P])

            def window(u, a):
                hp, g = divmod(u, 4)
                v = rpb_win[:, 2 * hp, (ROWS - 1) * RPB_C + 31 - BIAS_AT[KIND[g]][a]:]
                return bass.AP(v.tensor, v.offset, [list(v.ap[0]), [BSEG, 2], [-RPB_C, ROWS], [-1, 16]])

            def col_mask(u, a):
                v = cst[:, C_MASK + 32 * KIND[u % 4] + 16 * a:]
                return bass.AP(v.tensor, v.offset, [list(v.ap[0]), [0, 2], [0, ROWS], [1, 16]])

            def by_chunk(v, a):
                return v.rearrange("p (j a r x) -> p j a r x", j=2, a=2, r=ROWS)[:, :, a]

            def normalise(u):
                b = u % 2
                dve.wait_ge(exped, 2 * (u + 1))
                link(nc.vector.reciprocal(rsum[b], ssum[b]))
                for j in range(2):
                    last = nc.vector.tensor_scalar(pr[b][:, j, :], pr[b][:, j, :], rsum[b][:, j:j + 1], None, ALU.mult)
                last.then_inc(probs_ready, 1)

            def taps(m):
                y, u = yT[:, 4 + m, :], uT[:, m, :]
                dve.wait_ge(proj_kept[(PJ_H + m) % 2], (PJ_H + m) // 2 + 1)
                link(nc.vector.tensor_scalar(y, u, cw[:, 1, m:m + 1], None, ALU.mult))
                link(nc.vector.scalar_tensor_tensor(y[:, 1:S], u[:, 0:S - 1], cw[:, 0, m:m + 1], y[:, 1:S], ALU.mult, ALU.add))
                link(nc.vector.scalar_tensor_tensor(y[:, 0:S - 1], u[:, 1:S], cw[:, 2, m:m + 1], y[:, 0:S - 1], ALU.mult, ALU.add))

            dve.wait_ge(small_in, 64)
            dve.wait_ge(rpb_in, 16 * ROWS)
            dve.wait_ge(cst_in, 16)
            for u in range(NU):
                b = u % 2
                dve.wait_ge(scored, u + 1)
                if u >= 2:
                    dve.wait_ge(exped, 2 * (u - 1))
                flat = sc[b].rearrange("p j n -> p (j n)")
                for a in range(2):
                    last = nc.vector.tensor_tensor(by_chunk(flat, a), by_chunk(ps[b][:, :], a), window(u, a), ALU.add)
                last.then_inc(scores_kept[b], 1)
                dve.wait_ge(scores_kept[b], u // 2 + 1)
                for a in range(2):
                    last = nc.vector.tensor_tensor(by_chunk(flat, a), by_chunk(flat, a), col_mask(u, a), ALU.add)
                link(last)
                nc.vector.tensor_reduce(nmax[b], sc[b], AX, ALU.max, negate=True).then_inc(maxed, 1)
                normalise(u)
                for n in FILL[u]:
                    if PJ_H <= n < PJ_B:
                        m = n - PJ_H
                        dve.wait_ge(projected, n + 1)
                        dve.wait_ge(proj_kept[(PJ_C + m) % 2], (PJ_C + m) // 2 + 1)
                        nc.vector.tensor_tensor(uT[:, m, :], pj[n % 2][:, :], uT[:, m, :], ALU.mult)\
                            .then_inc(proj_kept[n % 2], 1)
                    elif n >= PJ_B:
                        y = yT[:, 4 + n - PJ_B, :]
                        dve.wait_ge(projected, n + 1)
                        nc.vector.tensor_tensor(y, pj[n % 2][:, :], y, ALU.mult).then_inc(proj_kept[n % 2], 1)
                if 9 <= u < 13:
                    taps(u - 9)

            def norm(buf, t, nth):
                link(nc.vector.bn_aggr(mv, bn.rearrange("p a n -> p (a n)")))
                if nth:
                    dve.wait_ge(rstd_ready, nth)
                nc.vector.tensor_scalar(var_eps, mv[:, 1:2], EPS, None, ALU.add).then_inc(var_ready, 1)
                dve.wait_ge(ln_in, 32 * (nth // TT + 1))
                row = buf[:, t, :]
                nc.vector.scalar_tensor_tensor(row, row, mv[:, 0:1], ln[:, 0, :], ALU.subtract, ALU.mult).then_inc(gained, 1)
                dve.wait_ge(gained, nth + 1)
                if nth < 2 * TT or t == TT - 1:
                    dve.wait_ge(rstd_ready, nth + 1)
                    nc.vector.scalar_tensor_tensor(row, row, rstd(t), ln[:, 1, :], ALU.mult, ALU.add).then_inc(normed, 1)

            def add_half(first, t, a):
                n = first + 2 * t + a
                dve.wait_ge(projected, n + 1)
                r = res[:, t, 512 * a:512 * a + 512]
                nc.vector.scalar_tensor_tensor(r, r, ALPHA, pj[n % 2][:, :], ALU.mult, ALU.add)\
                    .then_inc(proj_kept[n % 2], 1)
                dve.wait_ge(proj_kept[n % 2], n // 2 + 1)
                link(nc.vector.bn_stats(bn[:, a, :], r))

            def add_and_norm(first, t, nth):
                for a in range(2):
                    add_half(first, t, a)
                norm(res, t, nth)

            for t in range(TT):
                add_and_norm(PJ_OUT, t, t)

            def mem_max(v):
                b = v % 2
                dve.wait_ge(scored, NU + v + 1)
                dve.wait_ge(exped, 2 * (NU + v - 1))
                link(nc.vector.tensor_reduce(nmax[b], ps[b][:, :].rearrange("p (j n) -> p j n", j=2), AX, ALU.max, negate=True))
                nc.vector.tensor_scalar(nmax[b], nmax[b], float(P) ** -0.5, None, ALU.mult).then_inc(maxed, 1)

            mem_max(0)
            mem_max(1)
            normalise(NU)
            for v in range(MU):
                t = (v - 4) // 2
                if v + 1 < MU:
                    normalise(NU + v + 1)
                if v in (4, 6):
                    add_half(PJ_MO, t, 0)
                    add_half(PJ_MO, t, 1)
                if v + 2 < MU:
                    mem_max(v + 2)
                if v in (5, 7):
                    norm(res, t, TT + t)
            for t in range(2, TT):
                add_and_norm(PJ_MO, t, TT + t)
            keep_turn(TN_X2 + 2 * TT - 1, xT[:, 4:8, P * (TT - 1):])

            lg = ps[0][:, 0:TT * E].rearrange("p (t e) -> p t e", t=TT)

            def per_tile(a):
                return bass.AP(a.tensor, a.offset, [list(a.ap[0]), [1, TT], [0, E]])

            dve.wait_ge(logits_done, 1)
            link(nc.vector.tensor_reduce(lmax, lg, AX, ALU.max))
            nc.vector.tensor_tensor(aff, lg, per_tile(lmax), ALU.subtract).then_inc(lmaxed, 1)
            dve.wait_ge(lexped, 1)
            link(nc.vector.tensor_reduce(lsum, aff, AX, ALU.add))
            link(nc.vector.reciprocal(lrec, lsum))
            nc.vector.tensor_tensor(aff, aff, per_tile(lrec), ALU.mult).then_inc(aff_ready, 1)
            dve.wait_ge(aff_ready, 1)
            nc.vector.tensor_copy(gate.rearrange("p i t e -> p t i e"), aff.rearrange("p t (i e) -> p t i e", e=2))
            dve.wait_ge(turned, TN_AFF + 1)
            nc.vector.tensor_copy(afft, pt[TN_AFF % 2][0:E, :]).then_inc(turn_kept[TN_AFF % 2], 1)
            dve.wait_ge(turn_kept[TN_AFF % 2], TN_AFF // 2 + 1)
            for _ in range(CAP // 8):
                link(nc.vector.max(top8, afft))
                link(nc.vector.match_replace(afft, top8, afft, -1.0))
            nc.vector.tensor_scalar(chosen, afft, 0.0, None, ALU.is_lt).then_inc(chosen_ready, 1)
            dve.wait_ge(turned, TN_MASK + 1)
            nc.vector.tensor_copy(mask_tok, pt[TN_MASK % 2][:, :].rearrange("p (t n) -> p t n", t=TT)[:, :, 0:E])\
                .then_inc(turn_kept[TN_MASK % 2], 1)
            flat_acc = y_acc.rearrange("p t d -> p (t d)")
            flat_res = res[:, :, :].rearrange("p t d -> p (t d)")
            for a, (s, n) in enumerate(((hid_ready, 2), (mix_kept, 1))):
                nc.vector.tensor_scalar(flat_acc[:, 2048 * a:2048 * a + 2048], flat_res[:, 2048 * a:2048 * a + 2048],
                                        ALPHA, None, ALU.mult).then_inc(s, n)
            dve.wait_ge(ranked, 1)
            dve.wait_ge(turn_kept[TN_MASK % 2], TN_MASK // 2 + 1)
            link(nc.vector.tensor_tensor(rank.rearrange("p i t e -> p t i e"),
                                         ps[1][:, 0:TT * E].rearrange("p (t i e) -> p t i e", t=TT, e=2),
                                         mask_tok.rearrange("p t (i e) -> p t i e", e=2), ALU.mult))

            ranks = cst[:, C_RANK:C_RANK + CAP]
            ranks = bass.AP(ranks.tensor, ranks.offset, [list(ranks.ap[0]), [0, 2 * TT], [1, CAP]])

            with dve.Fori(0, PAIRS) as i:
                def by_slot(a):
                    v = a[:, bass.ds(i, 1)]
                    return bass.AP(v.tensor, v.offset, [list(v.ap[0]), [1, 2 * TT], [0, CAP]])

                one = pick.rearrange("p t e n -> p (t e) n")
                one_g = pick_g.rearrange("p t e n -> p (t e) n")
                dve.wait_ge(mix_kept, i * MIX + 1)
                nc.vector.tensor_tensor(one, ranks, by_slot(rank), ALU.is_equal).then_inc(half_picked, 1)
                dve.wait_ge(half_picked, i + 1)
                nc.vector.tensor_tensor(one_g, one, by_slot(gate), ALU.mult).then_inc(picked, 1)
                for a in range(2):
                    dve.wait_ge(mixed, i * MIX + (a + 1))
                    nc.vector.tensor_copy(xeT[:, 4 * a:4 * a + 4, :], pv[a][:, :].rearrange("p (k n) -> p k n", k=4))\
                        .then_inc(mix_kept, 1)
                for e in range(2):
                    if e:
                        dve.wait_ge(mixed, i * MIX + 3)
                        nc.vector.tensor_copy(scat, pv[0][:, :].rearrange("p (t n) -> p t n", t=TT)).then_inc(mix_kept, 1)
                    for g in range(2):
                        dve.wait_ge(exp_used, i * CPP + (CPE * e + 4 * g + 4))
                        dve.wait_ge(silu_done, i * 4 + (2 * e + g + 1))
                        nc.vector.tensor_tensor(hid[g], bank[2 * g + 1][:, :], silu[g], ALU.mult).then_inc(hid_ready, 1)
                for c in range(2 * TT):
                    t, n = divmod(c, 2)
                    dve.wait_ge(mixed, i * MIX + (c + 4))
                    y = y_acc[:, t, 512 * n:512 * n + 512]
                    nc.vector.tensor_tensor(y, pv[(c + 1) % 2][:, :], y, ALU.add).then_inc(mix_kept, 1)

            dve.wait_ge(mix_kept, PAIRS * MIX + 1)
            for t in range(TT):
                for a in range(2):
                    last = nc.vector.bn_stats(bn[:, a, :], y_acc[:, t, 512 * a:512 * a + 512])
                link(last)
                norm(y_acc, t, 2 * TT + t)


def expert_in(pe, exp_in, i, j):
    pe.wait_ge(exp_in[(j + FIRST) % SLOTS], i * (16 * CPP // SLOTS) + 16 * (j // SLOTS + 1))


_INS = ["x", "mem", "w_in", "na_rpb", "conv_w", "w_mix_out", "ln1_g", "ln1_b", "w_mem_q", "w_mem_k", "w_mem_v",
        "w_mem_out", "ln2_g", "ln2_b", "w_router", "w_exp_gate", "w_exp_up", "w_exp_down", "ln3_g", "ln3_b"]


def kernel(**inputs):
    import concourse.bacc as bacc
    from concourse.bass_utils import run_bass_kernel_spmd

    nc = bacc.Bacc("TRN2", target_bir_lowering=False, num_devices=1)
    arrays, args = {}, []
    for name in _INS:
        a = inputs[name]
        if name == "na_rpb":
            a = np.flip(np.asarray(a), (2, 3))
        a = np.ascontiguousarray(a)
        arrays[f"in_{name}"] = a
        args.append(nc.dram_tensor(f"in_{name}", a.shape, F32, kind="ExternalInput").ap())
    arrays["shape_consts"] = shape_constants()
    args.append(nc.dram_tensor("shape_consts", [P, C_N], F32, kind="ExternalInput").ap())
    args.append(nc.dram_tensor("out_0", [1, S, D], F32, kind="ExternalOutput").ap())
    build(nc, *args)
    r = run_bass_kernel_spmd(nc, [arrays], core_ids=[0])
    return r.results[0]["out_0"]
```

```python
from contextlib import ExitStack

import concourse.bass as bass
import numpy as np
from concourse import mybir

F32 = mybir.dt.float32
F32R = mybir.dt.float32r
ALU = mybir.AluOpType
ACT = mybir.ActivationFunctionType
AX = mybir.AxisListType.X

P = 128
D, S, M = 1024, 512, 256
KT, TT, MT = D // P, S // P, M // P
GRID_W, ROWS = 64, S // 64
NAH, NAD = 8, 64
WIN_C = 16
RPB_R, RPB_C = 15, 31
MH = 4
E, CAP, FF = 16, 64, 2048
PAIRS = E // 2
ALPHA = float(2 ** 0.25)
EPS = 1e-5
FMIN = float(np.finfo(np.float32).min)
SLOT = 4096
SLOTS = 8
FIRST = 3
EXTRA = 8
EXTRAS = 2
CPE = 12
CPP = 2 * CPE
RPB_N = NAH * RPB_R * RPB_C
RPB_PAD = 8
BSEG = 256

C_ID, C_TRI, C_ONE, C_RANK, C_MASK = 0, 128, 256, 384, 448
C_N = C_MASK + 3 * 2 * 16


def shape_constants():
    c = np.zeros((P, C_N), np.float32)
    i = np.arange(P)
    c[:, C_ID:C_ID + P] = i[:, None] == i[None, :]
    c[:, C_TRI:C_TRI + P] = i[:, None] <= i[None, :]
    c[:, C_ONE:C_ONE + P] = 1
    c[:, C_RANK:C_RANK + CAP] = np.arange(1, CAP + 1)
    x = np.arange(16)
    cols = [np.where(x < 8, x, 48 + x)] + [16 * n - 8 + x for n in (1, 2, 3)]
    for kind, g in enumerate((0, 1, 3)):
        col = 16 * g + i % 16
        start = np.clip(col - WIN_C // 2, 0, GRID_W - WIN_C)
        for a in range(2):
            key = cols[(g + a) % 4]
            ok = (key[None, :] >= start[:, None]) & (key[None, :] < start[:, None] + WIN_C)
            c[:, C_MASK + (2 * kind + a) * 16:][:, :16] = np.where(ok, 0, FMIN)
    return c


KIND = (0, 1, 1, 2)
BIAS_AT = ((8, 16), (0, 16), (0, 8))

PJ_MK, PJ_MV, PJ_C, PJ_H, PJ_B, PJ_OUT, PJ_MQ, PJ_MO = 12, 16, 18, 22, 26, 30, 38, 46
TN_MEM, TN_V, TN_NA, TN_X1, TN_MP, TN_X2, TN_AFF, TN_MASK = 0, 4, 8, 24, 32, 40, 48, 49
NU = 16
MU = 8
FILL = [[12, 13], [14, 15], [16], [17]] + [[n] for n in range(PJ_C, PJ_OUT)]
CH_MK, CH_MV, CH_OUT, CH_MQ, CH_MO = 3, 4, 8, 10, 11
PRE_SLOT = (0, 1, 7, 0, 1, 7, 0, 1, 7, 0, 3, 5)
PIECES = 24
PIECE_CHUNK = [c for c in (0, 1, 2, 5, 6, 7) for _ in range(4)]
PIECE_PJ = list(range(12)) + list(range(PJ_C, PJ_OUT))
OUT_K = (4, 6, 0, 2)
OUT_ORDER = [(k + 4) % KT for k in range(KT)]
POOL_GROUPS, DVE_GROUPS = (0, 1, 4, 5), (2, 3, 6, 7)
OUT_SLOT = ((1, 2), (4, 5))
MQ_GROUPS = 4
MO_GROUPS = MH
STAT_TILES, SCALED_TILES = 3, 2
MIX = 3 + 8


def build(nc, x, mem, w_in, na_rpb, conv_w, w_mix_out, ln1_g, ln1_b, w_mem_q, w_mem_k, w_mem_v, w_mem_out,
          ln2_g, ln2_b, w_router, w_gate, w_up, w_down, ln3_g, ln3_b, consts, out):
    with ExitStack() as ctx:
        def sb(name, *shape):
            return ctx.enter_context(nc.sbuf_tensor(name, [P, *shape], F32))

        def sem(name):
            return ctx.enter_context(nc.semaphore(name))

        ring = sb("ring", SLOTS * SLOT)
        res = sb("res", TT, D)
        xT = sb("xT", KT, S)
        yt = sb("yt", SLOT)
        work = sb("work", 6 * 512)
        kv = sb("kv", 2048)
        ln = sb("ln", 2, D)
        cst = sb("cst", C_N)
        cw = sb("cw", 3, 4)
        wr = sb("wr", KT, E)
        stat = sb("stat", 96)

        def parts(name, tensor, at, *shape):
            return nc.alloc_sbuf_tensor_at(name, [P, *shape], F32R, offset=nc.lookup_mloc(tensor).addr + 4 * at)

        x_hi = parts("x_hi", xT, 0, KT, S)
        x_lo = parts("x_lo", ring, 3 * SLOT, KT, S)
        piece = parts("piece", ring, 2 * SLOT, 2, 2, KT, P)

        y_hi = parts("y_hi", yt, 0, KT, S)
        y_lo = parts("y_lo", ring, 6 * SLOT, KT, S)
        out_w = [[parts(f"out_w{n}{a}", ring, OUT_SLOT[n][a] * SLOT, 2, 4, 512) for a in range(2)] for n in range(2)]
        mq_w = [parts("mq_hi", ring, 7 * SLOT, KT, 512), parts("mq_lo", ring, 0, KT, 512)]
        o_hi = parts("o_hi", yt, 2048, MH, S)
        o_lo = parts("o_lo", xT, 0, MH, S)
        mo_w = [parts("mo_hi", ring, SLOT, MH, D), parts("mo_lo", ring, 2 * SLOT, MH, D)]

        na = ring[:, 4 * SLOT:]
        qz = na[:, 0:4096].rearrange("p (h t) -> p h t", h=NAH)
        kT = na[:, 4096:6144].rearrange("p (h t) -> p h t", h=4)
        vp = na[:, 6144:8192].rearrange("p (a n) -> p a n", a=4)
        memT = na[:, 8192:10240].rearrange("p (k m) -> p k m", k=KT)
        uT = na[:, 10240:12288].rearrange("p (m t) -> p m t", m=4)
        mem_tok = yt[:, 0:2048].rearrange("p (t d) -> p t d", t=MT)
        rpb_win = ln[:, :, :].rearrange("p a d -> p (a d)").rearrange("p (h n) -> p h n", h=NAH)
        taps_out = yt[:, 2048:4096].rearrange("p (m t) -> p m t", m=4)
        cq = yt[:, 0:2048].rearrange("p (h t) -> p h t", h=MH)
        sc = [work[:, 512 * b:512 * b + 512].rearrange("p (j n) -> p j n", j=2) for b in range(2)]
        pr = [work[:, 1024 + 512 * b:1536 + 512 * b].rearrange("p (j n) -> p j n", j=2) for b in range(2)]
        prT = [work[:, 2048 + 512 * b:2560 + 512 * b].rearrange("p (j n) -> p j n", j=4) for b in range(2)]
        kmT = kv[:, 0:1024].rearrange("p (h m) -> p h m", h=MH)
        vm = kv[:, 1024:2048].rearrange("p (a n) -> p a n", a=MT)
        ident = cst[:, C_ID:C_ID + P]

        y_acc = xT[:, :, :].rearrange("p k t -> p (k t)").rearrange("p (t d) -> p t d", t=TT)
        xeT = yt[:, 0:1024].rearrange("p (k n) -> p k n", k=KT)
        hidT = yt[:, 1024:1536].rearrange("p (s n) -> p s n", s=4)
        ye = yt[:, 1536:2560]
        scat = yt[:, 2560:3072].rearrange("p (t n) -> p t n", t=TT)
        pick = yt[:, 3072:3584].rearrange("p (t e n) -> p t e n", t=TT, e=2)
        pick_g = yt[:, 3584:4096].rearrange("p (t e n) -> p t e n", t=TT, e=2)
        silu = [work[:, 512 * b:512 * b + 512] for b in range(2)]
        hid = [work[:, 1024 + 512 * b:1536 + 512 * b] for b in range(2)]
        rank = kv[:, 0:64].rearrange("p (i t e) -> p i t e", i=PAIRS, t=TT)
        gate = kv[:, 64:128].rearrange("p (i t e) -> p i t e", i=PAIRS, t=TT)
        aff = kv[:, 128:192].rearrange("p (t e) -> p t e", t=TT)
        mask_tok = kv[:, 192:256].rearrange("p (t e) -> p t e", t=TT)
        afft, chosen, top8 = work[0:E, 0:512], work[0:E, 512:1024], work[0:E, 1024:1032]

        nmax = [stat[:, 2 * b:2 * b + 2] for b in range(2)]
        ssum = [stat[:, 4 + 2 * b:6 + 2 * b] for b in range(2)]
        rsum = [stat[:, 8 + 2 * b:10 + 2 * b] for b in range(2)]
        bn = stat[:, 12:24].rearrange("p (a n) -> p a n", a=2)
        mv = stat[:, 24:26]
        var_eps = stat[:, 26:27]
        neg_half = stat[:, 28:29]

        def rstd(t):
            return stat[:, 44 + t:45 + t]

        def minus_mean(t):
            return stat[:, 48 + t:49 + t]

        def row_sq(t):
            return stat[:, 53 + t:54 + t]

        row_sum = stat[:, 52:53]
        junk = work[:, 0:D]
        lmax = stat[:, 32:36]
        lsum = stat[:, 36:40]
        lrec = stat[:, 40:44]

        bank = [ctx.enter_context(nc.psum_tensor(f"bank{n}", [P, 512], F32)) for n in range(8)]
        pj, ps, pt, pv = bank[0:2], bank[2:4], bank[4:6], bank[6:8]
        px = pt + pv

        rpb_pad = nc.dram_tensor("rpb_pad", [RPB_N + 2 * RPB_PAD], F32, kind="Internal").ap()

        x_in = [sem(f"x_in{t}") for t in range(TT)]
        q_in = [sem(f"q_in{m}") for m in range(4)]
        ident_in, mem_in, cst_in, small_in = (sem(n) for n in ("ident_in", "mem_in", "cst_in", "small_in"))
        half_set = sem("half_set")
        rpb_padded, rpb_in = sem("rpb_padded"), sem("rpb_in")
        ln_in = sem("ln_in")
        pre_in = {s: sem(f"pre_in{s}") for s in sorted(set(PRE_SLOT))}
        x_turned, x_hi_kept, x_lo_kept = (sem(n) for n in ("x_turned", "x_hi_kept", "x_lo_kept"))
        hi_split, lo_split = sem("hi_split"), sem("lo_split")
        out_hi, out_lo_pool, out_lo_dve = sem("out_hi"), sem("out_lo_pool"), sem("out_lo_dve")
        mq_hi_split, mq_lo_split = sem("mq_hi_split"), sem("mq_lo_split")
        mo_hi_split, mo_lo_split, mem_hi = sem("mo_hi_split"), sem("mo_lo_split"), sem("mem_hi")
        att_hi, conv_gated, conv_hi, x1_hi = (sem(n) for n in ("att_hi", "conv_gated", "conv_hi", "x1_hi"))
        exp_in = [sem(f"exp_in{s}") for s in range(SLOTS)]
        extra_in = [sem(f"extra_in{n}") for n in range(EXTRAS)]
        half_in, y_started = sem("half_in"), sem("y_started")
        exp_used = sem("exp_used")
        turned = sem("turned")
        turn_kept = [sem(f"turn_kept{b}") for b in range(2)]
        projected = sem("projected")
        proj_kept = [sem(f"proj_kept{b}") for b in range(2)]
        scored = sem("scored")
        scores_kept = [sem(f"scores_kept{b}") for b in range(2)]
        pv_done = sem("pv_done")
        att_kept = [sem(f"att_kept{b}") for b in range(2)]
        zeroed, maxed, exped, probs_ready = (sem(n) for n in ("zeroed", "maxed", "exped", "probs_ready"))
        var_ready, gained, rstd_ready, normed, scaled, shifted, summed = (
            sem(n) for n in ("var_ready", "gained", "rstd_ready", "normed", "scaled", "shifted", "summed"))
        vec = sem("vec")
        logits_done, lmaxed, lexped, aff_ready, chosen_ready, ranked = (
            sem(n) for n in ("logits_done", "lmaxed", "lexped", "aff_ready", "chosen_ready", "ranked"))
        half_picked, picked, mixed, mix_kept = (sem(n) for n in ("half_picked", "picked", "mixed", "mix_kept"))
        silu_done, hid_ready, hid_turned, hidT_kept, ye_kept = (
            sem(n) for n in ("silu_done", "hid_ready", "hid_turned", "hidT_kept", "ye_kept"))
        stored = sem("stored")

        def cols512(w, n):
            return w.rearrange("(k p) n -> p k n", p=P)[:, :, 512 * n:512 * n + 512]

        win, wmo = w_in[0], w_mix_out[0]
        pre_src = [cols512(win, 0), cols512(win, 1), cols512(win, 2), cols512(w_mem_k[0], 0), cols512(w_mem_v[0], 0),
                   cols512(win, 4), cols512(win, 5), cols512(win, 3), cols512(wmo, 0), cols512(wmo, 1),
                   cols512(w_mem_q[0], 0), w_mem_out[0].rearrange("(k p) n -> p k n", p=P)]

        def pre_chunk(c):
            s = ring[:, PRE_SLOT[c] * SLOT:(PRE_SLOT[c] + 1) * SLOT]
            return s.rearrange("p (k n) -> p k n", k=4 if c == CH_MO else KT)

        def chunk_in(eng, c):
            eng.wait_ge(pre_in[PRE_SLOT[c]], 16 * PRE_SLOT[1:c + 1].count(PRE_SLOT[c]))

        def out_group(g):
            n, k = g // 4, OUT_K[g % 4]
            raw = pre_chunk(CH_OUT + n)[:, k:k + 2, :]
            w = out_w[n][0 if k >= 4 else 1]
            return raw, w[:, 0, k % 4:k % 4 + 2, :], w[:, 1, k % 4:k % 4 + 2, :]

        def raw_piece(p):
            return pre_chunk(PIECE_CHUNK[p])[:, :, P * (p % 4):P * (p % 4) + P]

        def exp_slot(j, first):
            return (j + FIRST - (0 if first and j < EXTRA else EXTRAS)) % SLOTS

        def exp_chunk(j, first):
            if first and j == EXTRA:
                return xT[:, :, :].rearrange("p k t -> p (k t)").rearrange("p (k n) -> p k n", k=4)
            s = exp_slot(j, first)
            return ring[:, s * SLOT:(s + 1) * SLOT].rearrange("p (k n) -> p k n", k=4)

        scattered = [(0, slice(0, 1024), work[:, 2048:3072]), (1, slice(0, 1024), ye), (2, slice(0, 1024), kv[:, 1024:2048]),
                     (3, slice(0, 512), yt[:, 2560:3072]), (3, slice(512, 1024), kv[:, 512:1024])]

        def exp_rhs(j, first, k, c):
            if first and j == EXTRA + 1:
                return scattered[k][2][:, 512 * c:512 * c + 512] if k < 3 else scattered[3 + c][2]
            return exp_chunk(j, first)[:, k, 512 * c:512 * c + 512]

        wg_v = w_gate[0].rearrange("e (k p) f -> e p k f", p=P)
        wu_v = w_up[0].rearrange("e (k p) f -> e p k f", p=P)
        wd_v = w_down[0].rearrange("e (k p) d -> e p k d", p=P)

        def exp_src(pair, j):
            e, n = 2 * pair + j // CPE, j % CPE
            if n < 8:
                g, w, k = n // 4, (wg_v, wu_v)[n % 2], 4 * (n % 4 // 2)
                return w[bass.ds(e, 1), :, k:k + 4, 1024 * g:1024 * g + 1024].rearrange("e p k f -> (e p) k f")
            k = 4 * (n - 8)
            return wd_v[bass.ds(e, 1), :, k:k + 4, :].rearrange("e p k d -> (e p) k d")

        def key_tokens(v, a):
            if a == 0:
                return v.rearrange("p (r g c) -> p r g c", r=ROWS, g=8)[:, :, 0:8:7, :]
            return v.rearrange("p (r c) -> p r c", r=ROWS)[:, :, 16 * a - 8:16 * a + 8]

        block = ctx.enter_context(nc.Block())

        @block.sync
        def _(sp):
            def load_pre(c):
                sp.dma_start(pre_chunk(c), pre_src[c]).then_inc(pre_in[PRE_SLOT[c]], 16)

            def load_exp(j, pair=0, first=True):
                landed = extra_in[0] if first and j == EXTRA else exp_in[exp_slot(j, first)]
                if j == CPP - 1:
                    for h, semaphore in enumerate((half_in, landed)):
                        sp.dma_start(exp_chunk(j, first)[:, 2 * h:2 * h + 2], exp_src(pair, j)[:, 2 * h:2 * h + 2])\
                            .then_inc(semaphore, 16)
                    return
                sp.dma_start(exp_chunk(j, first), exp_src(pair, j)).then_inc(landed, 16)

            sp.dma_start(cst[:, 0:C_TRI], consts[:, 0:C_TRI]).then_inc(ident_in, 16)
            for t in range(TT):
                sp.dma_start(res[:, t, :], x[0, P * t:P * t + P, :]).then_inc(x_in[t], 16)
            for m in range(4):
                sp.dma_start(raw_piece(m), pre_src[0][:, :, P * m:P * m + P]).then_inc(q_in[m], 16)
            load_pre(1)
            load_pre(2)
            sp.wait_ge(lo_split, 4)
            load_pre(CH_MK)
            sp.wait_ge(lo_split, 8)
            load_pre(CH_MV)
            sp.wait_ge(lo_split, 12)
            load_pre(5)
            sp.wait_ge(projected, PJ_MV)
            load_pre(6)
            sp.wait_ge(projected, PJ_C)
            load_pre(7)
            for c, done in ((CH_OUT, 16), (CH_OUT + 1, 20)):
                sp.wait_ge(lo_split, done)
                load_pre(c)
            sp.wait_ge(projected, PJ_OUT)
            load_pre(CH_MQ)
            sp.wait_ge(projected, PJ_MQ)
            load_pre(CH_MO)
            sp.wait_ge(mq_lo_split, MQ_GROUPS)
            load_exp(0)
            load_exp(1)
            sp.wait_ge(mo_lo_split, MO_GROUPS)
            load_exp(2)
            sp.wait_ge(projected, PJ_MO)
            for m in range(3, 6):
                load_exp(m)
            sp.wait_ge(projected, PJ_MO + 8)
            load_exp(6)
            load_exp(7)
            sp.wait_ge(logits_done, 1)
            load_exp(EXTRA)
            for row, cols, room in scattered:
                sp.dma_start(room, exp_src(0, EXTRA + 1)[:, row, cols]).then_inc(extra_in[1], 16)
            for j in range(EXTRA + EXTRAS, CPP):
                first_lot = j < EXTRA + EXTRAS + SLOTS
                sp.wait_ge(exp_used, j - SLOTS + 1 - (EXTRAS if first_lot else 0))
                load_exp(j)
            with sp.Fori(1, PAIRS) as i:
                for j in range(CPP):
                    sp.wait_ge(exp_used, i * CPP + (j - SLOTS + 1))
                    load_exp(j, i, first=False)
            for t in (0, 2, 1, 3):
                if t < SCALED_TILES:
                    sp.wait_ge(shifted, t + 1)
                else:
                    sp.wait_ge(normed, 2 * TT + t - SCALED_TILES + 1)
                sp.dma_start(out[0, P * t:P * t + P, :], y_acc[:, t, :]).then_inc(stored, 16)
            sp.wait_ge(stored, 16 * TT)

        @block.gpsimd
        def _(pool):
            nc.gpsimd.memset(neg_half, -0.5).then_inc(half_set, 1)
            for p in range(PIECES):
                pool.wait_ge(hi_split, p + 1)
                nc.gpsimd.tensor_tensor(piece[:, p % 2, 1, :, :], raw_piece(p), piece[:, p % 2, 0, :, :].bitcast(F32),
                                        ALU.subtract).then_inc(lo_split, 1)
            pool.wait_ge(half_set, 1)
            def inverse_std(n):
                if 0 <= n - 2 * TT < STAT_TILES:
                    pool.wait_ge(summed, 3 * (n - 2 * TT) + 3)
                    pool.wait_ge(rstd_ready, n)
                    nc.gpsimd.tensor_scalar(var_eps, row_sq(n - 2 * TT), 1.0 / D, EPS, ALU.mult, ALU.add).then_inc(var_ready, 1)
                pool.wait_ge(var_ready, n + 1)
                nc.gpsimd.tensor_tensor(rstd(n % TT), var_eps, neg_half, ALU.pow).then_inc(rstd_ready, 1)

            def add_b(t):
                pool.wait_ge(scaled, t + 1)
                y = y_acc[:, t, :]
                nc.gpsimd.tensor_tensor(y, y, ln[:, 1, :], ALU.add).then_inc(shifted, 1)

            for g in POOL_GROUPS:
                raw, hi, lo = out_group(g)
                pool.wait_ge(out_hi, g + 1)
                nc.gpsimd.tensor_tensor(lo, raw, hi.bitcast(F32), ALU.subtract).then_inc(out_lo_pool, 1)
            for n in range(3 * TT):
                if n == 2 * TT:
                    pool.wait_ge(exp_used, EXTRA + 1)
                    for a in range(2):
                        nc.gpsimd.tensor_scalar(y_acc[:, 2 * a:2 * a + 2, :], res[:, 2 * a:2 * a + 2, :], ALPHA, None,
                                                ALU.mult).then_inc(y_started, 1)
                if n == 3 * TT - 1:
                    for t in range(SCALED_TILES):
                        add_b(t)
                inverse_std(n)
                for g in range(2 * n, min(2 * n + 2, MQ_GROUPS)):
                    k = slice(2 * g, 2 * g + 2)
                    pool.wait_ge(mq_hi_split, g + 1)
                    nc.gpsimd.tensor_tensor(mq_w[1][:, k, :], pre_chunk(CH_MQ)[:, k, :], mq_w[0][:, k, :].bitcast(F32),
                                            ALU.subtract).then_inc(mq_lo_split, 1)
                if n == TT - 1:
                    for h in range(MO_GROUPS):
                        pool.wait_ge(mo_hi_split, h + 1)
                        nc.gpsimd.tensor_tensor(mo_w[1][:, h, :], pre_chunk(CH_MO)[:, h, :],
                                                mo_w[0][:, h, :].bitcast(F32), ALU.subtract).then_inc(mo_lo_split, 1)
        @block.scalar
        def _(act):
            def load_ln(g, b):
                act.dma_start(ln[:, 0, :], g.to_broadcast([P, D])).then_inc(ln_in, 16)
                act.dma_start(ln[:, 1, :], b.to_broadcast([P, D])).then_inc(ln_in, 16)

            def load_small():
                act.dma_start(mem_tok, mem[0].rearrange("(t p) d -> p t d", p=P)).then_inc(mem_in, 16)
                act.dma_start(cst[:, C_TRI:], consts[:, C_TRI:]).then_inc(cst_in, 16)
                flat = na_rpb[0].rearrange("h r c -> (h r c)")
                act.dma_start(rpb_pad[RPB_PAD:RPB_PAD + RPB_N], flat).then_inc(rpb_padded, 16)
                act.dma_start(rpb_pad[0:RPB_PAD], flat[0:RPB_PAD]).then_inc(rpb_padded, 16)
                act.dma_start(rpb_pad[RPB_PAD + RPB_N:], flat[0:RPB_PAD]).then_inc(rpb_padded, 16)
                with nc.allow_non_contiguous_dma(reason="a few per-channel scalars"):
                    for k in range(3):
                        act.dma_start(cw[:, k, :], conv_w[0, k].rearrange("(m p) -> p m", p=P)).then_inc(small_in, 16)
                act.dma_start(wr[:], w_router[0].rearrange("(k p) e -> p k e", p=P)).then_inc(small_in, 16)

            seg = (ROWS - 1) * RPB_C + 32
            def load_bias():
                act.wait_ge(rpb_padded, 48)
                for r in range(ROWS):
                    src = bass.AP(rpb_pad.tensor, RPB_C * r, [[1, 16], [RPB_R * RPB_C, NAH], [1, seg]])
                    act.dma_start(rpb_win[16 * r:16 * r + 16, :, 0:seg], src).then_inc(rpb_in, 16)

            def split(p):
                if p < 4:
                    act.wait_ge(q_in[p], 16)
                else:
                    chunk_in(act, PIECE_CHUNK[p])
                if p >= 2:
                    act.wait_ge(projected, PIECE_PJ[p - 2] + 1)
                nc.scalar.activation(piece[:, p % 2, 0, :, :], raw_piece(p), ACT.Copy).then_inc(hi_split, 1)

            def keep_turn(n, dst):
                act.wait_ge(turned, n + 1)
                nc.scalar.activation(dst, pt[n % 2][:, :].rearrange("p (a b) -> p a b", a=4), ACT.Copy)\
                    .then_inc(turn_kept[n % 2], 1)

            def keep_proj(n, dst, width=512):
                act.wait_ge(projected, n + 1)
                nc.scalar.activation(dst, pj[n % 2][:, 0:width], ACT.Copy).then_inc(proj_kept[n % 2], 1)

            for n in range(2 * TT):
                t, a = divmod(n, 2)
                act.wait_ge(x_turned, n + 1)
                nc.scalar.activation(x_hi[:, 4 * a:4 * a + 4, P * t:P * t + P],
                                     px[n % 4][:, :].rearrange("p (a b) -> p a b", a=4), ACT.Copy).then_inc(x_hi_kept, 1)
            split(0)
            split(1)
            load_small()
            for n in range(4):
                split(n + 2)
                if n == 0:
                    act.wait_ge(zeroed, 1)
                act.wait_ge(projected, n + 1)
                for j in range(2):
                    h = slice(64 * j, 64 * j + 64)
                    last = nc.scalar.activation(qz[h, 2 * n + j, :].rearrange("p (g r c) -> p g r c", g=4, r=ROWS),
                                                pj[n % 2][h, :].rearrange("p (r g c) -> p g r c", r=ROWS, g=4),
                                                ACT.Copy, scale=NAD ** -0.5)
                last.then_inc(proj_kept[n % 2], 1)
            load_bias()
            for n in range(4, 8):
                split(n + 2)
                keep_proj(n, kT[:, n - 4, :])
            for t in range(MT):
                keep_turn(TN_MEM + 2 * t, memT[:, 0:4, P * t:P * t + P])
            for m in range(4):
                n = 8 + m
                if m < 2:
                    split(n + 2)
                act.wait_ge(projected, n + 1)
                src = pj[n % 2]
                nc.scalar.activation(uT[:, m, 0:P].rearrange("p (r g c) -> p r g c", r=ROWS, g=2),
                                     key_tokens(src[:, :], 0), ACT.Copy)
                nc.scalar.activation(uT[:, m, P:S].rearrange("p (a r x) -> p a r x", a=3, r=ROWS),
                                     src[:, :].rearrange("p (r c) -> p r c", r=ROWS)[:, :, 8:56]
                                     .rearrange("p r (a x) -> p a r x", a=3), ACT.Copy).then_inc(proj_kept[n % 2], 1)
            for m in range(4):
                keep_turn(TN_V + m, vp[:, :, P * m:P * m + P])

            def keep_att(hp):
                act.wait_ge(pv_done, 4 * hp + 4)
                nc.scalar.activation(y_hi[:, hp, :].rearrange("p (r g c) -> p g r c", r=ROWS, g=4),
                                     pv[hp % 2][:, :].rearrange("p (g r c) -> p g r c", g=4, r=ROWS), ACT.Copy)\
                    .then_inc(att_hi, 1)

            def split_out(g):
                raw, hi, _ = out_group(g)
                nc.scalar.activation(hi, raw, ACT.Copy).then_inc(out_hi, 1)

            for u in range(NU):
                act.wait_ge(maxed, u + 1)
                if u >= 2:
                    act.wait_ge(turned, TN_NA + u - 1)
                for j in range(2):
                    nc.scalar.activation(pr[u % 2][:, j, :], sc[u % 2][:, j, :], ACT.Exp, bias=nmax[u % 2][:, j:j + 1],
                                         accum_out=ssum[u % 2][:, j:j + 1]).then_inc(exped, 1)
                if 4 <= u < NU - 2:
                    split(10 + u)
                for n in FILL[u]:
                    if n < PJ_MV:
                        keep_proj(n, kmT[:, n - PJ_MK, :], M)
                    elif n < PJ_C:
                        keep_proj(n, vm[:, n - PJ_MV, :])
                    elif n < PJ_H:
                        keep_proj(n, uT[:, n - PJ_C, :])
                    elif n >= PJ_B:
                        act.wait_ge(conv_gated, n - PJ_B + 1)
                        nc.scalar.activation(y_hi[:, 4 + n - PJ_B, :], pj[n % 2][:, :], ACT.Copy).then_inc(conv_hi, 1)
                if u >= 2:
                    act.wait_ge(pv_done, u - 1)
                keep_turn(TN_NA + u, prT[u % 2])
                if u in (1, 2):
                    split(11 + u)
                if u == NU - 2:
                    act.wait_ge(lo_split, PIECES)
                    chunk_in(act, CH_OUT)
                if u >= NU - 2:
                    split_out(u - (NU - 2))
                if u % 4 == 0 and u:
                    keep_att(u // 4 - 1)
            load_ln(ln1_g, ln1_b)
            act.wait_ge(projected, PJ_OUT)
            split_out(2)
            split_out(3)
            keep_att(3)
            chunk_in(act, CH_OUT + 1)
            for g in range(4, 8):
                split_out(g)
            chunk_in(act, CH_MQ)
            act.wait_ge(out_lo_pool, 2)
            act.wait_ge(out_lo_dve, 4)
            for g in range(MQ_GROUPS):
                k = slice(2 * g, 2 * g + 2)
                nc.scalar.activation(mq_w[0][:, k, :], pre_chunk(CH_MQ)[:, k, :], ACT.Copy).then_inc(mq_hi_split, 1)

            def keep_x1(t):
                for a in range(2):
                    n = TN_X1 + 2 * t + a
                    act.wait_ge(turned, n + 1)
                    nc.scalar.activation(x_hi[:, 4 * a:4 * a + 4, P * t:P * t + P],
                                         pt[n % 2][:, :].rearrange("p (a b) -> p a b", a=4), ACT.Copy).then_inc(x1_hi, 1)

            def mem_exp(v):
                b = v % 2
                act.wait_ge(maxed, NU + v + 1)
                act.wait_ge(turned, TN_MP + v - 1 if v >= 2 else TN_NA + NU)
                for j in range(2):
                    nc.scalar.activation(pr[b][:, j, :], ps[b][:, M * j:M * j + M], ACT.Exp,
                                         bias=nmax[b][:, j:j + 1], scale=float(P) ** -0.5,
                                         accum_out=ssum[b][:, j:j + 1]).then_inc(exped, 1)

            def keep_mem(v):
                t, hp = divmod(v, 2)
                act.wait_ge(pv_done, NU + v + 1)
                nc.scalar.activation(o_hi[:, 2 * hp:2 * hp + 2, P * t:P * t + P],
                                     pv[v % 2][:, 0:256].rearrange("p (j n) -> p j n", j=2), ACT.Copy)\
                    .then_inc(mem_hi, 1)

            for t in range(3):
                keep_x1(t)
            for h in range(MH):
                keep_proj(PJ_MQ + h, cq[:, h, 0:256], 256)
            keep_x1(3)
            mem_exp(0)
            mem_exp(1)
            chunk_in(act, CH_MO)
            for h in range(MH):
                keep_proj(PJ_MQ + 4 + h, cq[:, h, 256:512], 256)
                nc.scalar.activation(mo_w[0][:, h, :], pre_chunk(CH_MO)[:, h, :], ACT.Copy).then_inc(mo_hi_split, 1)
            act.wait_ge(normed, TT)
            load_ln(ln2_g, ln2_b)
            for v in range(MU):
                if v >= 2:
                    act.wait_ge(pv_done, NU + v - 1)
                keep_turn(TN_MP + v, prT[v % 2])
                if v + 2 < MU:
                    mem_exp(v + 2)
                if v:
                    keep_mem(v - 1)
            keep_mem(MU - 1)
            for n in range(2 * TT - 1):
                t, a = divmod(n, 2)
                keep_turn(TN_X2 + n, xT[:, 4 * a:4 * a + 4, P * t:P * t + P])
            act.wait_ge(normed, 2 * TT)
            load_ln(ln3_g, ln3_b)
            act.wait_ge(lmaxed, 1)
            nc.scalar.activation(aff, aff, ACT.Exp).then_inc(lexped, 1)

            with act.Fori(0, PAIRS) as i:
                for e in range(2):
                    for g in range(2):
                        act.wait_ge(exp_used, i * CPP + (CPE * e + 4 * g + 3))
                        nc.scalar.activation(silu[g], bank[2 * g][:, :], ACT.Silu).then_inc(silu_done, 1)
                    for g in range(2):
                        act.wait_ge(hid_turned, i * 4 + (2 * e + g + 1))
                        nc.scalar.activation(hidT, bank[4][:, :].rearrange("p (s n) -> p s n", s=4), ACT.Copy)\
                            .then_inc(hidT_kept, 1)
                    act.wait_ge(exp_used, i * CPP + CPE * (e + 1))
                    for n in range(2):
                        nc.scalar.activation(ye[64 * e:64 * e + 64, 512 * n:512 * n + 512],
                                             bank[5][64 * n:64 * n + 64, :], ACT.Copy).then_inc(ye_kept, 1)
            for t in range(STAT_TILES):
                act.wait_ge(mix_kept, PAIRS * MIX + 1 - 2 * (TT - 1 - t))
                if t:
                    act.wait_ge(summed, 3 * t)
                nc.scalar.activation(junk, y_acc[:, t, :], ACT.Copy, accum_out=row_sum).then_inc(summed, 1)
                act.wait_ge(summed, 3 * t + 1)
                nc.scalar.activation(minus_mean(t), row_sum, ACT.Copy, scale=-1.0 / D).then_inc(summed, 1)
                act.wait_ge(summed, 3 * t + 2)
                nc.scalar.activation(junk, y_acc[:, t, :], ACT.Square, bias=minus_mean(t), accum_out=row_sq(t))\
                    .then_inc(summed, 1)
            for t in range(SCALED_TILES):
                act.wait_ge(gained, 2 * TT + t + 1)
                act.wait_ge(rstd_ready, 2 * TT + t + 1)
                nc.scalar.activation(y_acc[:, t, :], y_acc[:, t, :], ACT.Copy, scale=rstd(t)).then_inc(scaled, 1)

        @block.tensor
        def _(pe):
            def turn(n, blocks):
                if n >= 2:
                    pe.wait_ge(turn_kept[n % 2], n // 2)
                for a, (src, rows, cols) in enumerate(blocks):
                    mm = nc.tensor.transpose(pt[n % 2][0:cols, a * P:a * P + rows], src, ident[0:rows, 0:rows])
                mm.then_inc(turned, 1)

            def project(n, k, lhs, rhs, width=512):
                if n >= 2:
                    pe.wait_ge(proj_kept[n % 2], n // 2)
                for c in range(k):
                    mm = nc.tensor.matmul(pj[n % 2][:, 0:width], lhs(c), rhs(c), start=c == 0, stop=c == k - 1)
                mm.then_inc(projected, 1)

            def from_x(p):
                n = PIECE_PJ[p]
                hi, lo = piece[:, p % 2, 0], piece[:, p % 2, 1]
                if n >= 2:
                    pe.wait_ge(proj_kept[n % 2], n // 2)
                pe.wait_ge(hi_split, p + 1)
                for k in range(KT):
                    nc.tensor.matmul(pj[n % 2][:, :], hi[:, k, :], x_hi[:, k, :], start=k == 0, stop=False)
                for k in range(KT):
                    nc.tensor.matmul(pj[n % 2][:, :], hi[:, k, :], x_lo[:, k, :], start=False, stop=False)
                pe.wait_ge(lo_split, p + 1)
                for k in range(KT):
                    mm = nc.tensor.matmul(pj[n % 2][:, :], lo[:, k, :], x_hi[:, k, :], start=False, stop=k == KT - 1)
                mm.then_inc(projected, 1)

            def turns_kept(n):
                for b in range(2):
                    pe.wait_ge(turn_kept[b], n // 2 + 1)

            pe.wait_ge(ident_in, 16)
            for t in range(TT):
                pe.wait_ge(x_in[t], 16)
                for a in range(2):
                    n = 2 * t + a
                    if n >= 4:
                        pe.wait_ge(x_lo_kept, n - 3)
                    for k in range(4):
                        mm = nc.tensor.transpose(px[n % 4][:, P * k:P * k + P],
                                                 res[:, t, P * (4 * a + k):P * (4 * a + k) + P], ident)
                    mm.then_inc(x_turned, 1)
            pe.wait_ge(x_lo_kept, 2 * TT)
            for p in range(8):
                from_x(p)
            pe.wait_ge(mem_in, 16)
            for t in range(MT):
                for a in range(2):
                    turn(TN_MEM + 2 * t + a, [(mem_tok[:, t, P * k:P * k + P], P, P) for k in range(4 * a, 4 * a + 4)])
            for p in range(8, 12):
                from_x(p)
            for m in range(4):
                pe.wait_ge(proj_kept[m % 2], (8 + m) // 2 + 1)
                turn(TN_V + m, [(uT[:, m, P * a:P * a + P], P, P) for a in range(4)])

            def filler(n):
                if n >= PJ_C:
                    from_x(12 + n - PJ_C)
                elif n < PJ_MV:
                    m = n - PJ_MK
                    if m == 0:
                        turns_kept(TN_MEM + 3)
                        chunk_in(pe, CH_MK)
                    project(n, KT, lambda k: pre_chunk(CH_MK)[:, k, P * m:P * m + P], lambda k: memT[:, k, :], M)
                else:
                    t = n - PJ_MV
                    if t == 0:
                        chunk_in(pe, CH_MV)
                    project(n, KT, lambda k: memT[:, k, P * t:P * t + P], lambda k: pre_chunk(CH_MV)[:, k, :])

            def na_scores(u):
                hp, g = divmod(u, 4)
                if u == 0:
                    for b in range(2):
                        pe.wait_ge(proj_kept[b], 4)
                if u >= 2:
                    pe.wait_ge(scores_kept[u % 2], u // 2)
                for j in range(2):
                    q = qz[:, 2 * hp + j, P * g:P * g + P]
                    for a in range(2):
                        mm = nc.tensor.matmul(ps[u % 2][:, M * j + P * a:M * j + P * a + P], q,
                                              key_tokens(kT[:, hp, :], (g + a) % 4), start=True, stop=True)
                mm.then_inc(scored, 1)

            def na_pv(u):
                hp, g = divmod(u, 4)
                n = TN_NA + u
                pe.wait_ge(turn_kept[n % 2], n // 2 + 1)
                if u == 0:
                    turns_kept(TN_V + 3)
                if g == 0 and hp >= 2:
                    pe.wait_ge(att_kept[hp % 2], hp // 2)
                for j in range(2):
                    for a in range(2):
                        v = vp[:, (g + a) % 4, NAD * (2 * hp + j):NAD * (2 * hp + j) + NAD]
                        mm = nc.tensor.matmul(pv[hp % 2][64 * j:64 * j + 64, P * g:P * g + P], v,
                                              prT[u % 2][:, 2 * j + a, :], start=a == 0, stop=a == 1)
                mm.then_inc(pv_done, 1)

            def turn_probs(n, b, ready):
                pe.wait_ge(probs_ready, ready)
                turn(n, [(pr[b][:, j, P * a:P * a + P], P, P) for j in range(2) for a in range(2)])

            for u in range(NU):
                na_scores(u)
                for n in FILL[u]:
                    filler(n)
                turn_probs(TN_NA + u, u % 2, u + 1)
                if u:
                    na_pv(u - 1)
            na_pv(NU - 1)

            def mix_out(t):
                for c in range(2):
                    n = PJ_OUT + 2 * t + c
                    pe.wait_ge(proj_kept[n % 2], n // 2)
                    for i, k in enumerate(OUT_ORDER):
                        if t == 0 and i % 2 == 0:
                            g = 4 * c + i // 2
                            pe.wait_ge(out_hi, g + 1)
                            if g in POOL_GROUPS:
                                pe.wait_ge(out_lo_pool, POOL_GROUPS.index(g) + 1)
                            else:
                                pe.wait_ge(out_lo_dve, DVE_GROUPS.index(g) + 1)
                        if t == 0 and k == 3:
                            pe.wait_ge(att_kept[1], 2)
                        w = out_w[c][i // 4]
                        yh, yl = (y[:, k, P * t:P * t + P] for y in (y_hi, y_lo))
                        acc = pj[n % 2][:, :]
                        nc.tensor.matmul(acc, yh, w[:, 0, k % 4, :], start=i == 0, stop=False)
                        nc.tensor.matmul(acc, yh, w[:, 1, k % 4, :], start=False, stop=False)
                        mm = nc.tensor.matmul(acc, yl, w[:, 0, k % 4, :], start=False, stop=i == KT - 1)
                    mm.then_inc(projected, 1)

            def turn_res(first, t, done):
                pe.wait_ge(normed, done)
                for a in range(2):
                    turn(first + 2 * t + a, [(res[:, t, P * k:P * k + P], P, P) for k in range(4 * a, 4 * a + 4)])

            def mem_q(half):
                turns_kept(TN_X1 + 4 * half + 3)
                for h in range(MH):
                    n = PJ_MQ + 4 * half + h
                    pe.wait_ge(proj_kept[n % 2], n // 2)
                    for k in range(KT):
                        wh, wl = (w[:, k, P * h:P * h + P] for w in mq_w)
                        xh, xl = (x[:, k, 256 * half:256 * half + 256] for x in (x_hi, y_lo))
                        acc = pj[n % 2][:, 0:256]
                        nc.tensor.matmul(acc, wh, xh, start=k == 0, stop=False)
                        nc.tensor.matmul(acc, wh, xl, start=False, stop=False)
                        mm = nc.tensor.matmul(acc, wl, xh, start=False, stop=k == KT - 1)
                    mm.then_inc(projected, 1)

            pe.wait_ge(att_kept[0], 2)
            pe.wait_ge(att_kept[1], 1)
            for b in range(2):
                pe.wait_ge(proj_kept[b], PJ_OUT // 2)
            mix_out(0)
            mix_out(1)
            turn_res(TN_X1, 0, 1)
            mix_out(2)
            turn_res(TN_X1, 1, 2)
            mix_out(3)
            turn_res(TN_X1, 2, 3)
            pe.wait_ge(mq_lo_split, MQ_GROUPS)
            mem_q(0)

            def mem_scores(v):
                t, hp = divmod(v, 2)
                n = PJ_MQ + 4 * (t // 2) + 3
                for b in range(2):
                    pe.wait_ge(proj_kept[b], n // 2 + 1)
                if v < 2:
                    pe.wait_ge(scores_kept[v % 2], NU // 2)
                else:
                    pe.wait_ge(exped, 2 * (NU + v - 1))
                for j in range(2):
                    h = 2 * hp + j
                    mm = nc.tensor.matmul(ps[v % 2][:, M * j:M * j + M], cq[:, h, P * t:P * t + P], kmT[:, h, :],
                                          start=True, stop=True)
                mm.then_inc(scored, 1)

            def mem_pv(v):
                t, hp = divmod(v, 2)
                n = TN_MP + v
                pe.wait_ge(turn_kept[n % 2], n // 2 + 1)
                pe.wait_ge(att_kept[v % 2], 2 + v // 2)
                for j in range(2):
                    for a in range(2):
                        mm = nc.tensor.matmul(pv[v % 2][:, P * j:P * j + P], vm[:, a, P * (2 * hp + j):P * (2 * hp + j) + P],
                                              prT[v % 2][:, 2 * j + a, :], start=a == 0, stop=a == 1)
                mm.then_inc(pv_done, 1)

            def mem_out(t):
                if t == 0:
                    pe.wait_ge(mo_lo_split, MO_GROUPS)
                for b in range(2):
                    pe.wait_ge(att_kept[b], 2 + t + 1)
                for c in range(2):
                    n = PJ_MO + 2 * t + c
                    pe.wait_ge(proj_kept[n % 2], n // 2)
                    for h in range(MH):
                        oh, ol = (o[:, h, P * t:P * t + P] for o in (o_hi, o_lo))
                        wh, wl = (w[:, h, 512 * c:512 * c + 512] for w in mo_w)
                        acc = pj[n % 2][:, :]
                        nc.tensor.matmul(acc, oh, wh, start=h == 0, stop=False)
                        nc.tensor.matmul(acc, oh, wl, start=False, stop=False)
                        mm = nc.tensor.matmul(acc, ol, wh, start=False, stop=h == MH - 1)
                    mm.then_inc(projected, 1)

            turn_res(TN_X1, 3, 4)
            mem_scores(0)
            mem_scores(1)
            mem_q(1)
            for v in range(MU):
                turn_probs(TN_MP + v, v % 2, NU + v + 1)
                if v + 2 < MU:
                    mem_scores(v + 2)
                if v:
                    mem_pv(v - 1)
                if v in (3, 5, 7):
                    mem_out((v - 3) // 2)
            mem_pv(MU - 1)
            turn_res(TN_X2, 0, TT + 1)
            mem_out(3)

            pe.wait_ge(exped, 2 * (NU + MU))
            pe.wait_ge(small_in, 64)
            pe.wait_ge(cst_in, 16)
            for t in range(TT):
                if t + 1 < TT:
                    turn_res(TN_X2, t + 1, TT + t + 2)
                turns_kept(TN_X2 + 2 * t + 1)
                for k in range(KT):
                    mm = nc.tensor.matmul(ps[0][:, E * t:E * t + E], xT[:, k, P * t:P * t + P], wr[:, k, :],
                                          start=k == 0, stop=k == KT - 1)
            mm.then_inc(logits_done, 1)
            pe.wait_ge(aff_ready, 1)
            turn(TN_AFF, [(aff[:, t, :], P, E) for t in range(TT)])
            pe.wait_ge(chosen_ready, 1)
            turn(TN_MASK, [(chosen[:, P * t:P * t + P], E, P) for t in range(TT)])
            pe.wait_ge(turn_kept[TN_MASK % 2], TN_MASK // 2 + 1)
            flat_mask = mask_tok.rearrange("p t e -> p (t e)")
            for back in range(TT):
                lhs = cst[:, C_ONE:C_ONE + P] if back else cst[:, C_TRI:C_TRI + P]
                mm = nc.tensor.matmul(ps[1][:, E * back:TT * E], lhs, flat_mask[:, 0:(TT - back) * E],
                                      start=back == 0, stop=back == TT - 1)
            mm.then_inc(ranked, 1)

            def gather(k0, k1):
                for k in range(k0, k1):
                    for t in range(TT):
                        mm = nc.tensor.matmul(pv[k // 4][:, P * (k % 4):P * (k % 4) + P], res[:, t, P * k:P * k + P],
                                              pick[:, t].rearrange("p e n -> p (e n)"), start=t == 0, stop=t == TT - 1)
                if k1 % 4 == 0:
                    mm.then_inc(mixed, 1)

            def expert_in(i, j, first):
                if first and EXTRA <= j < EXTRA + EXTRAS:
                    pe.wait_ge(extra_in[j - EXTRA], 16 * (1 if j == EXTRA else len(scattered)))
                elif first and j < EXTRA:
                    pe.wait_ge(exp_in[exp_slot(j, first)], 16)
                else:
                    pe.wait_ge(exp_in[exp_slot(j, first)], i * (16 * CPP // SLOTS) + 16 * ((j - EXTRA - EXTRAS) // SLOTS + 2))

            def pair(i, first):
                pe.wait_ge(half_picked, i + 1)
                pe.wait_ge(mix_kept, i * MIX + 1)
                gather(0, 4)
                gather(4, 5)
                for e in range(2):
                    if e:
                        pe.wait_ge(picked, i + 1)
                        for t in range(TT):
                            mm = nc.tensor.transpose(pv[0][:, P * t:P * t + P], pick_g[:, t].rearrange("p e n -> p (e n)"),
                                                     ident)
                        mm.then_inc(mixed, 1)
                    for g in range(2):
                        if not first or e:
                            pe.wait_ge(hid_ready, i * 4 + (2 * e + g - 1))
                        for n in range(4):
                            j = CPE * e + 4 * g + n
                            if j == 0:
                                pe.wait_ge(mix_kept, i * MIX + 2)
                            if j == 1:
                                gather(5, 8)
                            if j == 2:
                                pe.wait_ge(mix_kept, i * MIX + 3)
                            expert_in(i, j, first)
                            for k in range(4):
                                kk = 4 * (n // 2) + k
                                for c in range(2):
                                    mm = nc.tensor.matmul(bank[2 * g + n % 2][64 * c:64 * c + 64, :],
                                                          xeT[:, kk, 64 * e:64 * e + 64],
                                                          exp_rhs(j, first, k, c), start=kk == 0, stop=kk == KT - 1)
                            mm.then_inc(exp_used, 1)
                    if e:
                        pe.wait_ge(ye_kept, i * 4 + 2)
                    for g in range(2):
                        pe.wait_ge(hid_ready, i * 4 + (2 * e + g + 1))
                        for s in range(4):
                            mm = nc.tensor.transpose(bank[4][:, P * s:P * s + P], hid[g][:, P * s:P * s + P], ident)
                        mm.then_inc(hid_turned, 1)
                        pe.wait_ge(hidT_kept, i * 4 + (2 * e + g + 1))
                        for c in range(2):
                            j = CPE * e + 8 + 2 * g + c
                            if j == CPP - 1:
                                pe.wait_ge(half_in, i * 16 + 16)
                            else:
                                expert_in(i, j, first)
                            for s in range(4):
                                if j == CPP - 1 and s == 2:
                                    expert_in(i, j, first)
                                for n in range(2):
                                    mm = nc.tensor.matmul(bank[5][64 * n:64 * n + 64, :], hidT[:, s, 64 * c:64 * c + 64],
                                                          exp_rhs(j, first, s, n),
                                                          start=(g, c, s) == (0, 0, 0), stop=(g, c, s) == (1, 1, 3))
                            mm.then_inc(exp_used, 1)
                for c in range(2 * TT):
                    t, n = divmod(c, 2)
                    if c < 2:
                        pe.wait_ge(ye_kept, i * 4 + (3 + c))
                    pe.wait_ge(mix_kept, i * MIX + (c + 3 if c else 4))
                    mm = nc.tensor.matmul(pv[(c + 1) % 2][:, :], scat[:, t, :], ye[:, 512 * n:512 * n + 512],
                                          start=True, stop=True)
                    mm.then_inc(mixed, 1)

            pair(0, first=True)
            with pe.Fori(1, PAIRS) as i:
                pair(i, first=False)

        @block.vector
        def _(dve):
            links = [0]

            def link(ins):
                links[0] += 1
                ins.then_inc(vec, 1)
                dve.wait_ge(vec, links[0])

            def keep_turn(n, dst):
                dve.wait_ge(turned, n + 1)
                nc.vector.tensor_copy(dst, pt[n % 2][:, :].rearrange("p (a b) -> p a b", a=4))\
                    .then_inc(turn_kept[n % 2], 1)

            nc.vector.memset(qz, 0.0).then_inc(zeroed, 1)
            for n in range(2 * TT):
                t, a = divmod(n, 2)
                hi = x_hi[:, 4 * a:4 * a + 4, P * t:P * t + P].bitcast(F32)
                dve.wait_ge(x_hi_kept, n + 1)
                nc.vector.tensor_tensor(x_lo[:, 4 * a:4 * a + 4, P * t:P * t + P],
                                        px[n % 4][:, :].rearrange("p (a b) -> p a b", a=4), hi, ALU.subtract)\
                    .then_inc(x_lo_kept, 1)
            for t in range(MT):
                keep_turn(TN_MEM + 2 * t + 1, memT[:, 4:8, P * t:P * t + P])

            def window(u, a):
                hp, g = divmod(u, 4)
                v = rpb_win[:, 2 * hp, (ROWS - 1) * RPB_C + 31 - BIAS_AT[KIND[g]][a]:]
                return bass.AP(v.tensor, v.offset, [list(v.ap[0]), [BSEG, 2], [-RPB_C, ROWS], [-1, 16]])

            def col_mask(u, a):
                v = cst[:, C_MASK + 32 * KIND[u % 4] + 16 * a:]
                return bass.AP(v.tensor, v.offset, [list(v.ap[0]), [0, 2], [0, ROWS], [1, 16]])

            def by_chunk(v, a):
                return v.rearrange("p (j a r x) -> p j a r x", j=2, a=2, r=ROWS)[:, :, a]

            def normalise(u):
                b = u % 2
                dve.wait_ge(exped, 2 * (u + 1))
                link(nc.vector.reciprocal(rsum[b], ssum[b]))
                for j in range(2):
                    last = nc.vector.tensor_scalar(pr[b][:, j, :], pr[b][:, j, :], rsum[b][:, j:j + 1], None, ALU.mult)
                last.then_inc(probs_ready, 1)

            def taps(m):
                y, u = taps_out[:, m, :], uT[:, m, :]
                dve.wait_ge(proj_kept[(PJ_H + m) % 2], (PJ_H + m) // 2 + 1)
                link(nc.vector.tensor_scalar(y, u, cw[:, 1, m:m + 1], None, ALU.mult))
                link(nc.vector.scalar_tensor_tensor(y[:, 1:S], u[:, 0:S - 1], cw[:, 0, m:m + 1], y[:, 1:S], ALU.mult, ALU.add))
                link(nc.vector.scalar_tensor_tensor(y[:, 0:S - 1], u[:, 1:S], cw[:, 2, m:m + 1], y[:, 0:S - 1], ALU.mult, ALU.add))

            def att_low(hp):
                def grid(v):
                    return v.rearrange("p (r g c) -> p g r c", r=ROWS, g=4)

                dve.wait_ge(att_hi, hp + 1)
                src = pv[hp % 2][:, :].rearrange("p (g r c) -> p g r c", g=4, r=ROWS)
                nc.vector.tensor_tensor(grid(y_lo[:, hp, :]), src, grid(y_hi[:, hp, :].bitcast(F32)), ALU.subtract)\
                    .then_inc(att_kept[hp % 2], 1)

            dve.wait_ge(small_in, 64)
            dve.wait_ge(rpb_in, 16 * ROWS)
            dve.wait_ge(cst_in, 16)
            for u in range(NU):
                b = u % 2
                dve.wait_ge(scored, u + 1)
                if u >= 2:
                    dve.wait_ge(exped, 2 * (u - 1))
                flat = sc[b].rearrange("p j n -> p (j n)")
                for a in range(2):
                    last = nc.vector.tensor_tensor(by_chunk(flat, a), by_chunk(ps[b][:, :], a), window(u, a), ALU.add)
                last.then_inc(scores_kept[b], 1)
                dve.wait_ge(scores_kept[b], u // 2 + 1)
                for a in range(2):
                    last = nc.vector.tensor_tensor(by_chunk(flat, a), by_chunk(flat, a), col_mask(u, a), ALU.add)
                link(last)
                nc.vector.tensor_reduce(nmax[b], sc[b], AX, ALU.max, negate=True).then_inc(maxed, 1)
                normalise(u)
                for n in FILL[u]:
                    if PJ_H <= n < PJ_B:
                        m = n - PJ_H
                        dve.wait_ge(projected, n + 1)
                        dve.wait_ge(proj_kept[(PJ_C + m) % 2], (PJ_C + m) // 2 + 1)
                        nc.vector.tensor_tensor(uT[:, m, :], pj[n % 2][:, :], uT[:, m, :], ALU.mult)\
                            .then_inc(proj_kept[n % 2], 1)
                    elif n >= PJ_B:
                        dve.wait_ge(projected, n + 1)
                        nc.vector.tensor_tensor(pj[n % 2][:, :], pj[n % 2][:, :], taps_out[:, n - PJ_B, :], ALU.mult)\
                            .then_inc(conv_gated, 1)
                if 9 <= u < 13:
                    taps(u - 9)
                if u % 4 == 1 and u > 1:
                    att_low(u // 4 - 1)
                for n in FILL[u]:
                    if n >= PJ_B:
                        dve.wait_ge(conv_hi, n - PJ_B + 1)
                        nc.vector.tensor_tensor(y_lo[:, 4 + n - PJ_B, :], pj[n % 2][:, :],
                                                y_hi[:, 4 + n - PJ_B, :].bitcast(F32), ALU.subtract)\
                            .then_inc(proj_kept[n % 2], 1)
            for g in DVE_GROUPS:
                raw, hi, lo = out_group(g)
                dve.wait_ge(out_hi, g + 1)
                nc.vector.tensor_tensor(lo, raw, hi.bitcast(F32), ALU.subtract).then_inc(out_lo_dve, 1)
                if g == 3:
                    att_low(3)

            def norm(buf, t, nth):
                link(nc.vector.bn_aggr(mv, bn.rearrange("p a n -> p (a n)")))
                if nth:
                    dve.wait_ge(rstd_ready, nth)
                nc.vector.tensor_scalar(var_eps, mv[:, 1:2], EPS, None, ALU.add).then_inc(var_ready, 1)
                dve.wait_ge(ln_in, 32 * (nth // TT + 1))
                row = buf[:, t, :]
                nc.vector.scalar_tensor_tensor(row, row, mv[:, 0:1], ln[:, 0, :], ALU.subtract, ALU.mult).then_inc(gained, 1)
                dve.wait_ge(gained, nth + 1)
                dve.wait_ge(rstd_ready, nth + 1)
                nc.vector.scalar_tensor_tensor(row, row, rstd(t), ln[:, 1, :], ALU.mult, ALU.add).then_inc(normed, 1)

            def add_half(first, t, a):
                n = first + 2 * t + a
                dve.wait_ge(projected, n + 1)
                r = res[:, t, 512 * a:512 * a + 512]
                nc.vector.scalar_tensor_tensor(r, r, ALPHA, pj[n % 2][:, :], ALU.mult, ALU.add)\
                    .then_inc(proj_kept[n % 2], 1)
                dve.wait_ge(proj_kept[n % 2], n // 2 + 1)
                link(nc.vector.bn_stats(bn[:, a, :], r))

            def x1_low(t):
                for a in range(2):
                    n = TN_X1 + 2 * t + a
                    dve.wait_ge(x1_hi, 2 * t + a + 1)
                    nc.vector.tensor_tensor(y_lo[:, 4 * a:4 * a + 4, P * t:P * t + P],
                                            pt[n % 2][:, :].rearrange("p (a b) -> p a b", a=4),
                                            x_hi[:, 4 * a:4 * a + 4, P * t:P * t + P].bitcast(F32), ALU.subtract)\
                        .then_inc(turn_kept[n % 2], 1)

            for t in range(TT):
                for a in range(2):
                    add_half(PJ_OUT, t, a)
                norm(res, t, t)
                if t:
                    x1_low(t - 1)
            x1_low(TT - 1)

            def mem_max(v):
                b = v % 2
                dve.wait_ge(scored, NU + v + 1)
                dve.wait_ge(exped, 2 * (NU + v - 1))
                link(nc.vector.tensor_reduce(nmax[b], ps[b][:, :].rearrange("p (j n) -> p j n", j=2), AX, ALU.max, negate=True))
                nc.vector.tensor_scalar(nmax[b], nmax[b], float(P) ** -0.5, None, ALU.mult).then_inc(maxed, 1)

            mem_max(0)
            mem_max(1)
            def mem_low(v):
                t, hp = divmod(v, 2)
                at = (slice(None), slice(2 * hp, 2 * hp + 2), slice(P * t, P * t + P))
                dve.wait_ge(mem_hi, v + 1)
                nc.vector.tensor_tensor(o_lo[at], pv[v % 2][:, 0:256].rearrange("p (j n) -> p j n", j=2),
                                        o_hi[at].bitcast(F32), ALU.subtract).then_inc(att_kept[v % 2], 1)

            normalise(NU)
            for v in range(MU):
                t = (v - 4) // 2
                if v + 1 < MU:
                    normalise(NU + v + 1)
                if v >= MU - 2:
                    mem_low(v - 1)
                if v in (4, 6):
                    add_half(PJ_MO, t, 0)
                    add_half(PJ_MO, t, 1)
                if v + 2 < MU:
                    mem_max(v + 2)
                if 0 < v < MU - 2:
                    mem_low(v - 1)
                if v in (5, 7):
                    norm(res, t, TT + t)
            mem_low(MU - 1)
            for t in range(2, TT):
                for a in range(2):
                    add_half(PJ_MO, t, a)
                norm(res, t, TT + t)
            keep_turn(TN_X2 + 2 * TT - 1, xT[:, 4:8, P * (TT - 1):])

            lg = ps[0][:, 0:TT * E].rearrange("p (t e) -> p t e", t=TT)

            def per_tile(a):
                return bass.AP(a.tensor, a.offset, [list(a.ap[0]), [1, TT], [0, E]])

            dve.wait_ge(logits_done, 1)
            link(nc.vector.tensor_reduce(lmax, lg, AX, ALU.max))
            nc.vector.tensor_tensor(aff, lg, per_tile(lmax), ALU.subtract).then_inc(lmaxed, 1)
            dve.wait_ge(lexped, 1)
            link(nc.vector.tensor_reduce(lsum, aff, AX, ALU.add))
            link(nc.vector.reciprocal(lrec, lsum))
            nc.vector.tensor_tensor(aff, aff, per_tile(lrec), ALU.mult).then_inc(aff_ready, 1)
            dve.wait_ge(aff_ready, 1)
            nc.vector.tensor_copy(gate.rearrange("p i t e -> p t i e"), aff.rearrange("p t (i e) -> p t i e", e=2))\
                .then_inc(mix_kept, 1)
            dve.wait_ge(turned, TN_AFF + 1)
            nc.vector.tensor_copy(afft, pt[TN_AFF % 2][0:E, :]).then_inc(turn_kept[TN_AFF % 2], 1)
            dve.wait_ge(turn_kept[TN_AFF % 2], TN_AFF // 2 + 1)
            for _ in range(CAP // 8):
                link(nc.vector.max(top8, afft))
                link(nc.vector.match_replace(afft, top8, afft, -1.0))
            nc.vector.tensor_scalar(chosen, afft, 0.0, None, ALU.is_lt).then_inc(chosen_ready, 1)
            dve.wait_ge(turned, TN_MASK + 1)
            nc.vector.tensor_copy(mask_tok, pt[TN_MASK % 2][:, :].rearrange("p (t n) -> p t n", t=TT)[:, :, 0:E])\
                .then_inc(turn_kept[TN_MASK % 2], 1)
            dve.wait_ge(ranked, 1)
            dve.wait_ge(turn_kept[TN_MASK % 2], TN_MASK // 2 + 1)
            link(nc.vector.tensor_tensor(rank.rearrange("p i t e -> p t i e"),
                                         ps[1][:, 0:TT * E].rearrange("p (t i e) -> p t i e", t=TT, e=2),
                                         mask_tok.rearrange("p t (i e) -> p t i e", e=2), ALU.mult))

            ranks = cst[:, C_RANK:C_RANK + CAP]
            ranks = bass.AP(ranks.tensor, ranks.offset, [list(ranks.ap[0]), [0, 2 * TT], [1, CAP]])

            with dve.Fori(0, PAIRS) as i:
                def by_slot(a):
                    v = a[:, bass.ds(i, 1)]
                    return bass.AP(v.tensor, v.offset, [list(v.ap[0]), [1, 2 * TT], [0, CAP]])

                one = pick.rearrange("p t e n -> p (t e) n")
                one_g = pick_g.rearrange("p t e n -> p (t e) n")
                dve.wait_ge(mix_kept, i * MIX + 1)
                nc.vector.tensor_tensor(one, ranks, by_slot(rank), ALU.is_equal).then_inc(half_picked, 1)
                dve.wait_ge(half_picked, i + 1)
                nc.vector.tensor_tensor(one_g, one, by_slot(gate), ALU.mult).then_inc(picked, 1)
                for a in range(2):
                    dve.wait_ge(mixed, i * MIX + (a + 1))
                    nc.vector.tensor_copy(xeT[:, 4 * a:4 * a + 4, :], pv[a][:, :].rearrange("p (k n) -> p k n", k=4))\
                        .then_inc(mix_kept, 1)
                for e in range(2):
                    if e:
                        dve.wait_ge(mixed, i * MIX + 3)
                        nc.vector.tensor_copy(scat, pv[0][:, :].rearrange("p (t n) -> p t n", t=TT)).then_inc(mix_kept, 1)
                    for g in range(2):
                        dve.wait_ge(exp_used, i * CPP + (CPE * e + 4 * g + 4))
                        dve.wait_ge(silu_done, i * 4 + (2 * e + g + 1))
                        nc.vector.tensor_tensor(hid[g], bank[2 * g + 1][:, :], silu[g], ALU.mult).then_inc(hid_ready, 1)
                dve.wait_ge(y_started, 2)
                for c in range(2 * TT):
                    t, n = divmod(c, 2)
                    dve.wait_ge(mixed, i * MIX + (c + 4))
                    y = y_acc[:, t, 512 * n:512 * n + 512]
                    nc.vector.tensor_tensor(y, pv[(c + 1) % 2][:, :], y, ALU.add).then_inc(mix_kept, 1)

            dve.wait_ge(mix_kept, PAIRS * MIX + 1)
            for t in range(TT):
                row, n = y_acc[:, t, :], 2 * TT + t
                if t >= STAT_TILES:
                    for a in range(2):
                        last = nc.vector.bn_stats(bn[:, a, :], y_acc[:, t, 512 * a:512 * a + 512])
                    link(last)
                    link(nc.vector.bn_aggr(mv, bn.rearrange("p a n -> p (a n)")))
                    dve.wait_ge(rstd_ready, n)
                    nc.vector.tensor_scalar(var_eps, mv[:, 1:2], EPS, None, ALU.add).then_inc(var_ready, 1)
                    dve.wait_ge(ln_in, 32 * 3)
                    nc.vector.scalar_tensor_tensor(row, row, mv[:, 0:1], ln[:, 0, :], ALU.subtract, ALU.mult)\
                        .then_inc(gained, 1)
                else:
                    dve.wait_ge(summed, 3 * t + 3)
                    dve.wait_ge(ln_in, 32 * 3)
                    nc.vector.scalar_tensor_tensor(row, row, minus_mean(t), ln[:, 0, :], ALU.add, ALU.mult)\
                        .then_inc(gained, 1)
                if t >= SCALED_TILES:
                    dve.wait_ge(gained, n + 1)
                    dve.wait_ge(rstd_ready, n + 1)
                    nc.vector.scalar_tensor_tensor(row, row, rstd(t), ln[:, 1, :], ALU.mult, ALU.add).then_inc(normed, 1)


_INS = ["x", "mem", "w_in", "na_rpb", "conv_w", "w_mix_out", "ln1_g", "ln1_b", "w_mem_q", "w_mem_k", "w_mem_v",
        "w_mem_out", "ln2_g", "ln2_b", "w_router", "w_exp_gate", "w_exp_up", "w_exp_down", "ln3_g", "ln3_b"]


def kernel(**inputs):
    import concourse.bacc as bacc
    from concourse.bass_utils import run_bass_kernel_spmd

    nc = bacc.Bacc("TRN2", target_bir_lowering=False, num_devices=1)
    arrays, args = {}, []
    for name in _INS:
        a = inputs[name]
        if name == "na_rpb":
            a = np.flip(np.asarray(a), (2, 3))
        a = np.ascontiguousarray(a)
        arrays[f"in_{name}"] = a
        args.append(nc.dram_tensor(f"in_{name}", a.shape, F32, kind="ExternalInput").ap())
    arrays["shape_consts"] = shape_constants()
    args.append(nc.dram_tensor("shape_consts", [P, C_N], F32, kind="ExternalInput").ap())
    args.append(nc.dram_tensor("out_0", [1, S, D], F32, kind="ExternalOutput").ap())
    build(nc, *args)
    r = run_bass_kernel_spmd(nc, [arrays], core_ids=[0])
    return r.results[0]["out_0"]
```
